# Optimizing a Trainium2 kernel written in Bass

```python
import math
import jax, jax.numpy as jnp
from jax import lax
import numpy as np

D_MODEL = 1024
BATCH = 1
SEQ = 256
DEPTH = 1

N_MEM = 256
MOBA_HEADS = 8
MOBA_HD = 64
MOBA_W = MOBA_HEADS * MOBA_HD
MOBA_BLOCK = 256
MOBA_TOPK = 3
MOBA_QCHUNK = 32
HG_HEADS = 8
HG_DK = 64
HG_DV = 64
HG_W = HG_HEADS * HG_DK
HG_CHUNK = 64
MIX_W = MOBA_W + HG_HEADS * HG_DV
IN_COLS = 3 * MOBA_W + 4 * HG_W
X_HEADS = 4
X_HD = D_MODEL // X_HEADS
N_EXPERTS = 32
TOP_K = 4
D_FF = D_MODEL
SWIGLU_LIMIT = 7.0
SWIGLU_ALPHA = 1.702
MOE_BLOCK = 256
EPS = 1e-6
NEG = -1e30

kernel_name = 'hymba_moba_hgrn2_moe_layer'

def rmsnorm(x, g):
    xf = x.astype(jnp.float32)
    y = xf * lax.rsqrt(jnp.mean(xf * xf, axis=-1, keepdims=True) + EPS)
    return (y * g.astype(jnp.float32)).astype(x.dtype)

def split_heads(t, n_heads):
    b, s, w = t.shape
    return t.reshape(b, s, n_heads, w // n_heads).transpose(0, 2, 1, 3)

def moba_attention(q, k, v):
    B, H, S, hd = q.shape
    nb = -(-S // MOBA_BLOCK)
    pad = nb * MOBA_BLOCK - S
    kp = jnp.pad(k, ((0, 0), (0, 0), (0, pad), (0, 0)))
    vp = jnp.pad(v, ((0, 0), (0, 0), (0, pad), (0, 0)))
    kb = kp.reshape(B, H, nb, MOBA_BLOCK, hd)
    vb = vp.reshape(B, H, nb, MOBA_BLOCK, hd)
    kbar = jnp.mean(kb.astype(jnp.float32), axis=3)
    gate = jnp.einsum('bhsd,bhnd->bhsn', q.astype(jnp.float32), kbar)
    q_blk = jnp.arange(S, dtype=jnp.int32) // MOBA_BLOCK
    past = jnp.arange(nb, dtype=jnp.int32)[None, :] < q_blk[:, None]
    gate = jnp.where(past, gate, NEG)
    n_sel = min(MOBA_TOPK, nb)
    _, idx = lax.top_k(gate, n_sel)
    valid = idx < q_blk[:, None]

    nqc = S // MOBA_QCHUNK
    def to_chunks(t):
        return jnp.moveaxis(t.reshape(B, H, nqc, MOBA_QCHUNK, *t.shape[3:]), 2, 0)
    q_ch, idx_ch, val_ch = to_chunks(q), to_chunks(idx), to_chunks(valid)
    bi = jnp.arange(B)[:, None, None, None]
    hi = jnp.arange(H)[None, :, None, None]
    scale = hd ** -0.5

    def one_chunk(args):
        c, qc, ic, vc = args
        q0 = c * MOBA_QCHUNK
        j = q0 // MOBA_BLOCK
        k_sel = kb[bi, hi, ic]
        v_sel = vb[bi, hi, ic]
        k_own = lax.dynamic_index_in_dim(kb, j, axis=2, keepdims=False)
        v_own = lax.dynamic_index_in_dim(vb, j, axis=2, keepdims=False)
        s_sel = jnp.einsum('bhqd,bhqnkd->bhqnk', qc, k_sel).astype(jnp.float32) * scale
        s_sel = jnp.where(vc[..., None], s_sel, NEG).reshape(B, H, MOBA_QCHUNK, n_sel * MOBA_BLOCK)
        s_own = jnp.einsum('bhqd,bhkd->bhqk', qc, k_own).astype(jnp.float32) * scale
        qpos = q0 + jnp.arange(MOBA_QCHUNK, dtype=jnp.int32)
        kpos = j * MOBA_BLOCK + jnp.arange(MOBA_BLOCK, dtype=jnp.int32)
        s_own = jnp.where(kpos[None, :] <= qpos[:, None], s_own, NEG)
        p = jax.nn.softmax(jnp.concatenate([s_sel, s_own], axis=-1), axis=-1).astype(v.dtype)
        p_sel = p[..., :n_sel * MOBA_BLOCK].reshape(B, H, MOBA_QCHUNK, n_sel, MOBA_BLOCK)
        p_own = p[..., n_sel * MOBA_BLOCK:]
        return (jnp.einsum('bhqnk,bhqnkd->bhqd', p_sel, v_sel)
                + jnp.einsum('bhqk,bhkd->bhqd', p_own, v_own))

    out = lax.map(one_chunk, (jnp.arange(nqc, dtype=jnp.int32), q_ch, idx_ch, val_ch))
    return jnp.moveaxis(out, 0, 2).reshape(B, H, S, hd)

def hgrn2(q_raw, f_raw, i_raw, lb):
    B, S, _ = q_raw.shape
    f = lb + (1.0 - lb) * jax.nn.sigmoid(f_raw.astype(jnp.float32))
    logf = jnp.log(f)
    k = 1.0 - f
    q = jax.nn.silu(q_raw.astype(jnp.float32))
    v = i_raw.astype(jnp.float32)
    nch = S // HG_CHUNK
    def to_chunks(t):
        t = split_heads(t, HG_HEADS)
        return jnp.moveaxis(t.reshape(B, HG_HEADS, nch, HG_CHUNK, t.shape[-1]), 2, 0)
    qc, kc, vc, lc = to_chunks(q), to_chunks(k), to_chunks(v), to_chunks(logf)
    bc = jnp.cumsum(lc, axis=-2)
    tri = jnp.arange(HG_CHUNK)[:, None] >= jnp.arange(HG_CHUNK)[None, :]

    def step(state, inp):
        qt, kt, vt, bt = inp
        o_inter = jnp.einsum('bhtk,bhkv->bhtv', qt * jnp.exp(bt), state)
        diff = bt[:, :, :, None, :] - bt[:, :, None, :, :]
        decay = jnp.exp(jnp.where(tri[:, :, None], diff, -jnp.inf))
        a = jnp.einsum('bhtk,bhsk,bhtsk->bhts', qt, kt, decay)
        o_intra = jnp.einsum('bhts,bhsv->bhtv', a, vt)
        b_end = bt[:, :, -1]
        new_state = (jnp.exp(b_end)[..., None] * state
                     + jnp.einsum('bhsk,bhsv->bhkv', kt * jnp.exp(b_end[:, :, None] - bt), vt))
        return new_state, o_inter + o_intra

    s0 = jnp.zeros((B, HG_HEADS, HG_DK, HG_DV), jnp.float32)
    _, o = lax.scan(step, s0, (qc, kc, vc, bc))
    return jnp.moveaxis(o, 0, 2).reshape(B, HG_HEADS, S, HG_DV)

def cross_attention(hn, mem, g_mem, wq, wkv, wo):
    mn = rmsnorm(mem, g_mem)
    q = split_heads(hn @ wq, X_HEADS)
    k, v = jnp.split(mn @ wkv, 2, axis=-1)
    k, v = split_heads(k, X_HEADS), split_heads(v, X_HEADS)
    s = jnp.einsum('bhqd,bhkd->bhqk', q, k).astype(jnp.float32) * (X_HD ** -0.5)
    p = jax.nn.softmax(s, axis=-1).astype(v.dtype)
    o = jnp.einsum('bhqk,bhkd->bhqd', p, v)
    B, _, S, _ = o.shape
    return o.transpose(0, 2, 1, 3).reshape(B, S, D_MODEL) @ wo

def moe_ffn(xn, w_router, b_router, w1, b1, w2, b2):
    B, S, D = xn.shape
    T = B * S
    xt = xn.reshape(T, D)
    logits = (xt @ w_router).astype(jnp.float32) + b_router.astype(jnp.float32)
    top_v, top_i = lax.top_k(logits, TOP_K)
    gates = jax.nn.softmax(top_v, axis=-1)
    M = T * TOP_K
    flat_e = top_i.reshape(M)
    flat_tok = jnp.repeat(jnp.arange(T, dtype=jnp.int32), TOP_K)
    flat_g = gates.reshape(M)
    order = jnp.argsort(flat_e)
    se = flat_e[order]
    counts = jnp.zeros((N_EXPERTS,), jnp.int32).at[flat_e].add(1)
    start = jnp.cumsum(counts) - counts
    padded = (counts + MOE_BLOCK - 1) // MOE_BLOCK * MOE_BLOCK
    pad_end = jnp.cumsum(padded)
    pad_start = pad_end - padded
    dest = pad_start[se] + (jnp.arange(M, dtype=jnp.int32) - start[se])
    m_pad = M + N_EXPERTS * MOE_BLOCK
    n_blk = m_pad // MOE_BLOCK
    row_tok = jnp.zeros((m_pad,), jnp.int32).at[dest].set(flat_tok[order])
    row_g = jnp.zeros((m_pad,), jnp.float32).at[dest].set(flat_g[order])
    block_e = jnp.minimum(
        jnp.searchsorted(pad_end, jnp.arange(n_blk, dtype=jnp.int32) * MOE_BLOCK, side='right'),
        N_EXPERTS - 1).astype(jnp.int32)
    xs = xt[row_tok].reshape(n_blk, MOE_BLOCK, D)

    def expert_block(args):
        xb, e = args
        hcat = xb @ w1[e] + b1[e]
        glu = jnp.minimum(hcat[:, 0::2], SWIGLU_LIMIT)
        lin = jnp.clip(hcat[:, 1::2], -SWIGLU_LIMIT, SWIGLU_LIMIT)
        act = glu * jax.nn.sigmoid(SWIGLU_ALPHA * glu) * (lin + 1.0)
        return act @ w2[e] + b2[e]

    ys = lax.map(expert_block, (xs, block_e)).reshape(m_pad, D)
    out = jnp.zeros((T, D), jnp.float32).at[row_tok].add(ys.astype(jnp.float32) * row_g[:, None])
    return out.astype(xn.dtype).reshape(B, S, D)

def setup_inputs(seed: int = 0) -> dict:
    key = jax.random.key(seed)
    ks = jax.random.split(key, 24)
    f32 = jnp.float32
    def nrm(k, shape, scale):
        return jax.random.normal(k, shape, f32) * scale
    def gain(k, shape):
        return 1.0 + 0.02 * jax.random.normal(k, shape, f32)
    L = DEPTH
    return {
        'x': nrm(ks[0], (BATCH, SEQ, D_MODEL), 1.0),
        'mem': nrm(ks[1], (BATCH, N_MEM, D_MODEL), 1.0),
        'ln_mix_g': gain(ks[2], (L, D_MODEL)),
        'w_in': nrm(ks[3], (L, D_MODEL, IN_COLS), D_MODEL ** -0.5),
        'hgrn_lb_logits': nrm(ks[4], (L + 1, HG_W), 0.1),
        'hgrn_norm_g': gain(ks[5], (L, HG_HEADS * HG_DV)),
        'w_out': nrm(ks[6], (L, MIX_W, D_MODEL), MIX_W ** -0.5),
        'ln_x_g': gain(ks[7], (L, D_MODEL)),
        'ln_mem_g': gain(ks[8], (L, D_MODEL)),
        'wq_x': nrm(ks[9], (L, D_MODEL, D_MODEL), D_MODEL ** -0.5),
        'wkv_x': nrm(ks[10], (L, D_MODEL, 2 * D_MODEL), D_MODEL ** -0.5),
        'wo_x': nrm(ks[11], (L, D_MODEL, D_MODEL), D_MODEL ** -0.5),
        'ln_moe_g': gain(ks[12], (L, D_MODEL)),
        'w_router': nrm(ks[13], (L, D_MODEL, N_EXPERTS), D_MODEL ** -0.5),
        'b_router': nrm(ks[14], (L, N_EXPERTS), 0.01),
        'w1': nrm(ks[15], (L, N_EXPERTS, D_MODEL, 2 * D_FF), D_MODEL ** -0.5),
        'b1': nrm(ks[16], (L, N_EXPERTS, 2 * D_FF), 0.02),
        'w2': nrm(ks[17], (L, N_EXPERTS, D_FF, D_MODEL), D_FF ** -0.5),
        'b2': nrm(ks[18], (L, N_EXPERTS, D_MODEL), 0.02),
        'ln_f_g': gain(ks[19], (D_MODEL,)),
    }

def reference(x, mem, ln_mix_g, w_in, hgrn_lb_logits, hgrn_norm_g, w_out,
              ln_x_g, ln_mem_g, wq_x, wkv_x, wo_x,
              ln_moe_g, w_router, b_router, w1, b1, w2, b2, ln_f_g):
    B, S, _ = x.shape
    lb_table = jnp.cumsum(jax.nn.softmax(hgrn_lb_logits.astype(jnp.float32), axis=0), axis=0)
    split_pts = [MOBA_W, 2 * MOBA_W, 3 * MOBA_W,
                 3 * MOBA_W + HG_W, 3 * MOBA_W + 2 * HG_W, 3 * MOBA_W + 3 * HG_W]
    h = x
    for l in range(DEPTH):
        hn = rmsnorm(h, ln_mix_g[l])
        proj = hn @ w_in[l]
        mq, mk, mv, gq, gf, gi, gg = jnp.split(proj, split_pts, axis=-1)
        moba_o = moba_attention(split_heads(mq, MOBA_HEADS), split_heads(mk, MOBA_HEADS),
                                split_heads(mv, MOBA_HEADS))
        moba_o = moba_o.transpose(0, 2, 1, 3).reshape(B, S, MOBA_W)
        hg_o = hgrn2(gq, gf, gi, lb_table[l])
        hg_o = hg_o.transpose(0, 2, 1, 3)
        hg_o = hg_o * lax.rsqrt(jnp.mean(hg_o * hg_o, axis=-1, keepdims=True) + EPS)
        hg_o = hg_o * hgrn_norm_g[l].astype(jnp.float32).reshape(HG_HEADS, HG_DV)
        hg_o = (hg_o.reshape(B, S, HG_HEADS * HG_DV)
                * jax.nn.silu(gg.astype(jnp.float32))).astype(x.dtype)
        h = h + jnp.concatenate([moba_o, hg_o], axis=-1) @ w_out[l]
        h = h + cross_attention(rmsnorm(h, ln_x_g[l]), mem, ln_mem_g[l], wq_x[l], wkv_x[l], wo_x[l])
        h = h + moe_ffn(rmsnorm(h, ln_moe_g[l]), w_router[l], b_router[l],
                        w1[l], b1[l], w2[l], b2[l])
    return rmsnorm(h, ln_f_g)


_drawn_inputs = setup_inputs


def setup_inputs(seed=0):
    import zlib

    import numpy as np

    out = dict(_drawn_inputs(seed))
    spreads = {}
    factors = {'ln_x_g': 4.079,
     'ln_mem_g': 3.271,
     'b1': 5.511,
     'b2': 28.156,
     'ln_f_g': 22.829,
     'ln_moe_g': 3.663,
     'b_router': 6.915}
    for name, (base, spread) in spreads.items():
        noise = np.random.default_rng([zlib.crc32(name.encode()), seed]).standard_normal(out[name].shape)
        drawn = base * np.exp(spread * noise) if base else spread * noise
        out[name] = __import__('jax').numpy.asarray(drawn.astype(out[name].dtype))
    for name, factor in factors.items():
        out[name] = (out[name] * factor).astype(out[name].dtype)
    return out
```

```python
import numpy as np

import concourse.bass as bass
from concourse import mybir
from contextlib import ExitStack

F32 = mybir.dt.float32
BF16 = mybir.dt.bfloat16
I32 = mybir.dt.int32
U32 = mybir.dt.uint32
ALU = mybir.AluOpType
ACT = mybir.ActivationFunctionType
AX_X = mybir.AxisListType.X

P = 128
D = 1024
KC = D // P
T = 256
TT = T // P
HD = 64
NH = 8
NPAIR = NH // 2
GW = 512
XH, XHD = 4, 256
NE, TOPK = 32, 4
SLOTS = 64
MAXBLK = T // SLOTS
LIMIT, ALPHA = 7.0, 1.702
EPS = 1e-6
MASKED = -1e30
UNIT = 2048
EXPERT_UNITS = 12
FRONT_PAIRS = 3
LEVELS = [64, 32, 16, 8, 4, 2, 1]
OFF, DIAG = len(LEVELS), len(LEVELS) + 1
NLEV = len(LEVELS) + 2

(G_F, G_Q, M_Q, M_K, M_V, G_I, G_G, X_K0, X_K1, X_V0, X_V1,
 W_O0, W_O1, X_Q0, X_Q1, C_O0, C_O1) = range(17)
FEATURE_GROUPS = (G_F, G_Q, M_Q, M_K, X_K0, X_K1, X_Q0, X_Q1)


def mixing_schedule():
    small = []
    for l in range(NLEV):
        small.append(("decay", l))
        small.append(("level", l))
    heads = []
    for i in range(NH + 2):
        if i < NH:
            heads.append(("score", i))
        if i >= 2:
            heads.append(("out", i - 2))
        if 1 <= i <= NH:
            heads.append(("turn", i - 1))
    filler = [("proj", g, j) for g in (M_V, G_I, G_G, X_K0, X_K1, X_V0, X_V1) for j in range(4)]
    order, level_at, head_at = [], 0, 0
    for n, f in enumerate(filler):
        order.append(f)
        while level_at < len(small) and level_at * 26 <= n * len(small):
            order.append(small[level_at])
            level_at += 1
        while n >= 4 and head_at < len(heads) and head_at * 22 <= (n - 4) * len(heads):
            order.append(heads[head_at])
            head_at += 1
    return order + small[level_at:] + heads[head_at:]


def build(nc, x, mem, ln_mix_g, w_in, hgrn_lb_logits, hgrn_norm_g, w_out, ln_x_g, ln_mem_g, wq_x,
          wkv_x, wo_x, ln_moe_g, w_router, b_router, w1, b1, w2, b2, ln_f_g, out):
    ctx = ExitStack()
    with ctx:
        def sb(name, shape, dt=F32):
            return ctx.enter_context(nc.sbuf_tensor(name, shape, dt))

        def sem(name):
            return ctx.enter_context(nc.semaphore(name))

        expert_ring = sb("expert_ring", [P, EXPERT_UNITS, UNIT])
        front_ring = sb("front_ring", [P, 2 * FRONT_PAIRS, UNIT])
        h = sb("h", [P, TT, D])
        hn = sb("hn", [P, TT, D])
        hnT = sb("hnT", [P, KC, T])
        KxT = sb("KxT", [P, KC, T])
        Vx = sb("Vx", [P, TT, D])
        qxT = sb("qxT", [P, KC, T])
        pbuf = sb("pbuf", [P, 1536])

        def scratch(slot, a=0, b=UNIT):
            return expert_ring[:, slot, a:b]
        mem_sb = scratch(0).rearrange("p (t d) -> p t d", t=TT)
        mixT = scratch(0).rearrange("p (c t) -> p c t", c=KC)
        memT = scratch(1).rearrange("p (c t) -> p c t", c=KC)
        mqT = scratch(2, 0, 1024).rearrange("p (c t) -> p c t", c=NPAIR)
        mkT = scratch(2, 1024).rearrange("p (c t) -> p c t", c=NPAIR)
        mv = scratch(3, 0, 1024).rearrange("p (t d) -> p t d", t=TT)
        gi = scratch(3, 1024).rearrange("p (t d) -> p t d", t=TT)
        sgate = scratch(4, 0, 1024)
        bsum = scratch(4, 1024)
        gq = scratch(5, 0, 1024)
        fgate = scratch(5, 1024)
        kgate = scratch(6, 0, 1024)
        tmp = scratch(6, 1024)
        factor = [scratch(7, 0, 1024), scratch(7, 1024)]
        factor_pad = scratch(8).rearrange("p (c j t) -> p c j t", c=NPAIR, j=2)
        mem_n = scratch(8).rearrange("p (t d) -> p t d", t=TT)
        squares = scratch(8)
        a_in = scratch(9)
        a_off = scratch(10, 0, 1024)
        lmask = scratch(10, 1024).bitcast(I32).rearrange("p (l t) -> p l t", l=8)
        mix = scratch(11).rearrange("p (t d) -> p t d", t=TT)

        ident = sb("ident", [P, P])
        ones = sb("ones", [P, P])
        before = sb("before", [P, P])
        cmask = sb("cmask", [P, 3, P])
        iota_i = sb("iota_i", [P, 2, P], I32)
        xor_f = sb("xor_f", [P, P])
        iota_s = sb("iota_s", [P, T])
        eps = sb("eps", [P, 1])
        gains = sb("gains", [P, 4, KC])
        hg_gain = sb("hg_gain", [P, NPAIR])
        lbl = sb("lbl", [P, 2, NPAIR])
        lb = sb("lb", [P, 6, NPAIR])
        ssq = sb("ssq", [P, TT])
        std = sb("std", [P, TT])
        rstd = sb("rstd", [P, TT])
        hg_ssq = sb("hg_ssq", [P, 2 * NH])
        hg_rstd = sb("hg_rstd", [P, 2 * NH])
        mx = sb("mx", [P, 2, TT])
        nmx = sb("nmx", [P, 2, TT])
        psum_row = sb("psum_row", [P, 2, TT])
        rinv = sb("rinv", [P, 2, TT])
        wr = sb("wr", [P, KC, NE])
        br = sb("br", [P, NE])
        logits = sb("logits", [P, TT, NE])
        elog = sb("elog", [P, TT, NE])
        top8 = sb("top8", [P, TT, 8])
        idx8 = sb("idx8", [P, TT, 8], U32)
        idx8f = sb("idx8f", [P, TT, 8])
        sel = sb("sel", [P, TT, NE])
        ntop = sb("ntop", [P, TT])
        gate_sum = sb("gate_sum", [P, TT])
        posm = sb("posm", [P, TT, NE + 1])
        tabf = sb("tabf", [1, 5, NE])
        tab = sb("tab", [1, 2, NE], I32)

        ring_row = front_ring[:, :, :].rearrange("p u n -> p (u n)")
        at = [0]

        def loop_buf(n):
            at[0] += n
            assert at[0] <= 2 * FRONT_PAIRS * UNIT
            return ring_row[:, at[0] - n:at[0]]
        b1_sb = loop_buf(2 * D)
        b2_sb = loop_buf(D)
        xn_part = [loop_buf(D).bitcast(BF16).rearrange("p (t d) -> p t d", t=TT) for _ in range(3)]
        xgT = loop_buf(KC * SLOTS).rearrange("p (c s) -> p c s", c=KC)
        xgT_more = loop_buf(KC * SLOTS).rearrange("p (c s) -> p c s", c=KC)
        glu, lin, sig, actb, y_sb = (loop_buf(GW) for _ in range(5))
        actT = loop_buf(GW).rearrange("p (q j s) -> p q j s", q=4, j=2)
        sgT = loop_buf(2 * T).rearrange("p (n t) -> p n t", n=2)
        pick_gated = loop_buf(TT * P).rearrange("p (t n s) -> p t n s", t=TT, n=2)
        pick = loop_buf(TT * SLOTS // 2).bitcast(BF16).rearrange("p (t s) -> p t s", t=TT)
        b1_pick = loop_buf(SLOTS)
        gates = loop_buf(TT * P).rearrange("p (t e) -> p t e", t=TT)
        gatesT = loop_buf(T).rearrange("p (t s) -> p t s", t=TT)
        res = Vx[:, :, :]
        lnf = KxT[:, 0:4, :].rearrange("p c t -> p (c t)")

        ps = ctx.enter_context(nc.psum_tensor("ps", [P, 8, 512], F32))

        def banks(a, b):
            return ps[:, a:b, :]

        x_loaded, mem_loaded = sem("x_loaded"), sem("mem_loaded")
        small_loaded = sem("small_loaded")
        router_loaded = sem("router_loaded")
        unit_loaded = [sem(f"unit_loaded{s}") for s in range(2 * FRONT_PAIRS)]
        expert_loaded = [sem(f"expert_loaded{s}") for s in range(EXPERT_UNITS)]
        bias_loaded, lnf_loaded, out_stored = sem("bias_loaded"), sem("lnf_loaded"), sem("out_stored")
        pool_chain, act_chain, dve_chain = sem("pool_chain"), sem("act_chain"), sem("dve_chain")
        consts_ready, masks_ready = sem("consts_ready"), sem("masks_ready")
        pads_zeroed, loop_zeroed = sem("pads_zeroed"), sem("loop_zeroed")
        rows_squared, std_ready, hn_ready = sem("rows_squared"), sem("std_ready"), sem("hn_ready")
        hn_turned, hnT_ready = sem("hn_turned"), sem("hnT_ready")
        group_done, group_kept = sem("group_done"), sem("group_kept")
        forget_kept, gate_ready, log_ready = sem("forget_kept"), sem("gate_ready"), sem("log_ready")
        lb_exp = sem("lb_exp")
        diff_ready, decay_ready = sem("diff_ready"), sem("decay_ready")
        factor_ready, pad_ready = sem("factor_ready"), sem("pad_ready")
        level_done, level_kept = sem("level_done"), sem("level_kept")
        score_done, score_kept, prob_ready = sem("score_done"), sem("score_kept"), sem("prob_ready")
        prob_turned, probT_ready = sem("prob_turned"), sem("probT_ready")
        head_done, head_kept, rinv_ready = sem("head_done"), sem("head_kept"), sem("rinv_ready")
        hg_done, hg_squared, hg_summed = sem("hg_done"), sem("hg_squared"), sem("hg_summed")
        hg_std, hg_mix_ready = sem("hg_std"), sem("hg_mix_ready")
        mix_turned, mixT_ready = sem("mix_turned"), sem("mixT_ready")
        residual_ready = sem("residual_ready")
        xs_done, xs_max, xs_prob, xs_scaled = sem("xs_done"), sem("xs_max"), sem("xs_prob"), sem("xs_scaled")
        xp_turned, xpT_ready = sem("xp_turned"), sem("xpT_ready")
        xo_done, xo_kept = sem("xo_done"), sem("xo_kept")
        router_done, router_max, router_exp, chosen = (
            sem("router_done"), sem("router_max"), sem("router_exp"), sem("chosen"))
        ranked, ranks_kept = sem("ranked"), sem("ranks_kept")
        gates_turned, gatesT_ready = sem("gates_turned"), sem("gatesT_ready")
        table_ready, parts_ready = sem("table_ready"), sem("parts_ready")
        pick_ready, pickg_ready, b1_pick_ready = sem("pick_ready"), sem("pickg_ready"), sem("b1_pick_ready")
        bias_added, gathered, xgT_ready = sem("bias_added"), sem("gathered"), sem("xgT_ready")
        up_done, glu_ready, sig_ready, act_ready = sem("up_done"), sem("glu_ready"), sem("sig_ready"), sem("act_ready")
        act_turned, actT_ready = sem("act_turned"), sem("actT_ready")
        pickg_turned, sgT_ready = sem("pickg_turned"), sem("sgT_ready")
        down_done, y_ready, scattered = sem("down_done"), sem("y_ready"), sem("scattered")
        unit_used = sem("unit_used")
        dve_loop, act_loop = sem("dve_loop"), sem("act_loop")
        m_pick, m_gathered, m_xgT, m_up, m_glu, m_sig, m_act = (
            sem(f"more_{n}") for n in ("pick", "gathered", "xgT", "up", "glu", "sig", "act"))
        m_turned, m_sgT, m_actturn, m_actT, m_down, m_y, m_scattered = (
            sem(f"more_{n}") for n in ("turned", "sgT", "actturn", "actT", "down", "y", "scattered"))
        m_dve, m_closed = sem("more_dve"), sem("more_closed")

        def linker(eng, s):
            n = [0]

            def link(ins):
                n[0] += 1
                ins.then_inc(s, 1)
                eng.wait_ge(s, n[0])
            return link

        order = mixing_schedule()
        level_order = list(range(NLEV))

        def group_weights(g):
            if g <= G_G:
                return w_in, {G_F: 4, G_Q: 3, M_Q: 0, M_K: 1, M_V: 2, G_I: 5, G_G: 6}[g] * GW
            if g <= X_V1:
                return wkv_x, (g - X_K0) * GW
            if g <= W_O1:
                return w_out, (g - W_O0) * GW
            if g <= X_Q1:
                return wq_x, (g - X_Q0) * GW
            return wo_x, (g - C_O0) * GW

        def group_unit(g, k):
            slot = 2 * (g % FRONT_PAIRS) + k // 4
            return front_ring[:, slot, (k % 4) * GW:(k % 4 + 1) * GW]

        def group_arrived(eng, g, half):
            eng.wait_ge(unit_loaded[2 * (g % FRONT_PAIRS) + half], 16 * (g // FRONT_PAIRS + 1))

        def mp(i):
            return pbuf[:, (i % 2) * 384:(i % 2 + 1) * 384]

        def mpT(i):
            return pbuf[:, 768 + (i % 2) * 384:768 + (i % 2 + 1) * 384]

        def xp(i):
            return pbuf[:, (i % 2) * 512:(i % 2 + 1) * 512].rearrange("p (t k) -> p t k", t=TT)
        xpT = pbuf[:, 1024:1536].rearrange("p (k q) -> p k q", k=TT)

        def blocks_of(ap, m):
            v = ap.rearrange("p (n two m) -> p n two m", two=2, m=m)
            return v[:, :, 0, :], v[:, :, 1, :]

        block = ctx.enter_context(nc.Block())

        @block.sync
        def _(sp):
            for g in range(C_O1 + 1):
                src, col = group_weights(g)
                if g >= FRONT_PAIRS:
                    sp.wait_ge(group_done, g - FRONT_PAIRS + 1)
                for half in range(2):
                    sp.dma_start(
                        front_ring[:, 2 * (g % FRONT_PAIRS) + half, :].rearrange("p (k n) -> p k n", k=4),
                        src[0, half * 512:(half + 1) * 512, col:col + GW].rearrange("(k p) n -> p k n", p=P),
                    ).then_inc(unit_loaded[2 * (g % FRONT_PAIRS) + half], 16)

            def load_expert(e, u):
                if u < 8:
                    dst, src = expert_ring[:, u, :], w1[0, e, u * P:(u + 1) * P, :]
                else:
                    dst = expert_ring[:, u, :].rearrange("p (a n) -> p a n", a=2)
                    src = w2[0, e, (u - 8) * 2 * P:(u - 7) * 2 * P, :].rearrange("(a p) n -> p a n", p=P)
                sp.dma_start(dst, src).then_inc(expert_loaded[u], 16)

            sp.wait_ge(residual_ready, 1)
            for u in range(EXPERT_UNITS):
                load_expert(0, u)
            with sp.Fori(1, NE) as e:
                for u in range(EXPERT_UNITS):
                    if u == 7:
                        sp.wait_ge(up_done, e)
                    elif u == EXPERT_UNITS - 1:
                        sp.wait_ge(down_done, e)
                    else:
                        sp.wait_ge(unit_used, (e - 1) * (EXPERT_UNITS - 2) + (u + 1 if u < 7 else u))
                    load_expert(e, u)

            sp.wait_ge(hnT_ready, 9)
            for t in range(TT):
                sp.dma_start(out[0, t * P:(t + 1) * P, :], res[:, t, :]).then_inc(out_stored, 16)
            sp.wait_ge(out_stored, 16 * TT)

        @block.gpsimd
        def _(pool):
            def step(ins, done, n):
                ins.then_inc(done, 1)
                pool.wait_ge(done, n)

            step(nc.gpsimd.memset(ident[:, :], 0.0), pool_chain, 1)
            step(nc.gpsimd.affine_select(out=ident[:, :], in_=ident[:, :], compare_op=ALU.not_equal, fill=1.0,
                                         base=0, pattern=[[-1, P]], channel_multiplier=1), consts_ready, 1)
            step(nc.gpsimd.memset(eps[:, :], EPS), consts_ready, 2)
            step(nc.gpsimd.memset(ones[:, :], 1.0), pool_chain, 2)
            step(nc.gpsimd.affine_select(out=before[:, :], in_=ones[:, :], compare_op=ALU.is_gt, fill=0.0,
                                         base=0, pattern=[[1, P]], channel_multiplier=-1), masks_ready, 1)
            step(nc.gpsimd.memset(cmask[:, :, :], 0.0), pool_chain, 3)
            for n, c in enumerate((0, 2)):
                step(nc.gpsimd.affine_select(out=cmask[:, c, :], in_=cmask[:, c, :], compare_op=ALU.is_ge,
                                             fill=MASKED, base=0, pattern=[[-1, P]],
                                             channel_multiplier=1), masks_ready, 2 + n)
            step(nc.gpsimd.iota(iota_i[:, 0, :], pattern=[[1, P]], base=0, channel_multiplier=0), masks_ready, 4)
            step(nc.gpsimd.iota(iota_i[:, 1, :], pattern=[[0, P]], base=0, channel_multiplier=1), masks_ready, 5)
            step(nc.gpsimd.iota(iota_s[:, :], pattern=[[1, T]], base=0, channel_multiplier=0,
                                allow_small_or_imprecise_dtypes=True), masks_ready, 6)
            step(nc.gpsimd.memset(posm[:, :, NE:NE + 1], -1.0), masks_ready, 7)
            pool.wait_ge(hn_turned, 4)
            for j in range(2):
                step(nc.gpsimd.memset(factor_pad[64 * j:64 * j + 64, :, 1 - j, :], 0.0), pads_zeroed, j + 1)
            pool.wait_ge(group_done, C_O1 + 1)
            zeroed = [b[p:p + n, :] for b in (b1_sb, b2_sb) for p, n in ((32, 32), (64, 64))]
            zeroed += [sgT[64 * n:64 * n + 64, 1 - n, :] for n in range(2)] + [gates]
            for n, rows in enumerate(zeroed):
                step(nc.gpsimd.memset(rows, 0.0), loop_zeroed, n + 1)
            pool.dma_start(b1_sb[0:NE, :], b1[0]).then_inc(bias_loaded, 16)
            pool.dma_start(b2_sb[0:NE, :], b2[0]).then_inc(bias_loaded, 16)
            pool.dma_start(lnf, ln_f_g.partition_broadcast(P)).then_inc(lnf_loaded, 16)
            pool.wait_ge(bias_loaded, 32)
            pool.wait_ge(lnf_loaded, 16)

        @block.scalar
        def _(act):
            link = linker(act, act_chain)
            act.dma_start(h[:, :, :], x[0].rearrange("(t p) d -> p t d", p=P)).then_inc(x_loaded, 16)
            with nc.allow_non_contiguous_dma("gains go to columns, a few KB in all"):
                for n, g in enumerate((ln_mix_g, ln_mem_g, ln_x_g, ln_moe_g)):
                    act.dma_start(gains[:, n, :], g[0].rearrange("(c p) -> p c", p=P)).then_inc(small_loaded, 16)
                for r in range(2):
                    act.dma_start(lbl[:, r, :], hgrn_lb_logits[r].rearrange("(c p) -> p c", p=P)).then_inc(small_loaded, 16)
                act.dma_start(hg_gain[:, :], hgrn_norm_g[0].rearrange("(c p) -> p c", p=P)).then_inc(small_loaded, 16)
            act.dma_start(mem_sb, mem[0].rearrange("(t p) d -> p t d", p=P)).then_inc(mem_loaded, 16)
            act.dma_start(wr[:, :, :], w_router[0].rearrange("(c p) e -> p c e", p=P)).then_inc(router_loaded, 16)
            act.dma_start(br[:, :], b_router[0].partition_broadcast(P)).then_inc(router_loaded, 16)

            def norm_stats(n, src, scratch_rows):
                if n >= 1:
                    act.wait_ge(hn_ready, 2 * n)
                for t in range(TT):
                    nc.scalar.activation(scratch_rows[:, t, :], src[:, t, :], ACT.Square,
                                         accum_out=ssq[:, t:t + 1]).then_inc(rows_squared, 1)
                act.wait_ge(rows_squared, TT * (n + 1))
                nc.scalar.activation(std[:, :], ssq[:, :], ACT.Sqrt, bias=eps[:, :],
                                     scale=1.0 / D).then_inc(std_ready, 1)

            act.wait_ge(consts_ready, 2)
            act.wait_ge(x_loaded, 16)
            norm_stats(0, h, hn)
            act.wait_ge(mem_loaded, 16)
            norm_stats(1, mem_sb, mem_n)
            act.wait_ge(lb_exp, 1)
            nc.scalar.activation(lb[:, 2:4, :], lb[:, 0:2, :], ACT.Exp).then_inc(lb_exp, 1)

            def keep_group(g, a, dst):
                act.wait_ge(group_done, g + 1)
                return nc.scalar.activation(dst, banks(a, a + 2).rearrange("p b n -> p (b n)"), ACT.Copy)

            act.wait_ge(group_done, G_F + 1)
            nc.scalar.activation(fgate, banks(0, 2).rearrange("p b n -> p (b n)"), ACT.Exp,
                                 scale=-1.0).then_inc(group_kept, 1)
            keep_group(G_Q, 2, gq).then_inc(group_kept, 1)
            act.wait_ge(group_kept, 2)
            nc.scalar.activation(tmp, gq, ACT.Exp, scale=-1.0).then_inc(gate_ready, 1)
            keep_group(M_Q, 0, mqT.rearrange("p c t -> p (c t)")).then_inc(group_kept, 1)
            act.wait_ge(log_ready, 1)
            nc.scalar.activation(tmp, fgate, ACT.Ln).then_inc(log_ready, 1)
            keep_group(M_K, 0, mkT.rearrange("p c t -> p (c t)")).then_inc(group_kept, 1)

            def decay_exp(l):
                act.wait_ge(diff_ready, l + 1)
                nc.scalar.activation(factor[l % 2], factor[l % 2], ACT.Exp).then_inc(decay_ready, 1)
            act.wait_ge(pads_zeroed, 2)
            decay_exp(0)
            for item in order:
                kind, i = item[0], item[1]
                if kind == "proj" and item[2] == 3:
                    if i in (M_V, G_I):
                        dst = {M_V: mv, G_I: gi}[i].rearrange("p t d -> p (t d)")
                        keep_group(i, 0, dst).then_inc(group_kept, 1)
                    elif i == G_G:
                        keep_group(i, 0, sgate).then_inc(group_kept, 1)
                        act.wait_ge(group_kept, G_G + 1)
                        nc.scalar.activation(tmp, sgate, ACT.Exp, scale=-1.0).then_inc(gate_ready, 1)
                    elif i in (X_K0, X_K1):
                        dst = KxT[:, 4 * (i - X_K0):4 * (i - X_K0) + 4, :].rearrange("p c t -> p (c t)")
                        keep_group(i, 0, dst).then_inc(group_kept, 1)
                    else:
                        act.wait_ge(group_done, i + 1)
                        nc.scalar.activation(Vx[:, :, (i - X_V0) * GW:(i - X_V0 + 1) * GW], banks(0, 2),
                                             ACT.Copy).then_inc(group_kept, 1)
                elif kind == "decay":
                    if i + 1 <= OFF:
                        decay_exp(i + 1)
                    if i != DIAG:
                        act.wait_ge(factor_ready, i + 1)
                        src = factor[i % 2]
                    else:
                        src = gq
                    if i >= 1:
                        act.wait_ge(level_done, 2 * i)
                    for j in range(2):
                        nc.scalar.activation(
                            factor_pad[64 * j:64 * j + 64, :, j, :],
                            src[64 * j:64 * j + 64, :].rearrange("p (c t) -> p c t", c=NPAIR),
                            ACT.Copy).then_inc(pad_ready, 1)
                elif kind == "score":
                    act.wait_ge(score_kept, i + 1)
                    if i >= 2:
                        act.wait_ge(rinv_ready, i - 1)
                    for t in range(TT):
                        row = mp(i)[:, 0:128] if t == 0 else mp(i)[:, 128:384]
                        nc.scalar.activation(row, row, ACT.Exp, bias=nmx[:, i % 2, t:t + 1],
                                             accum_out=psum_row[:, i % 2, t:t + 1]).then_inc(prob_ready, 1)
                elif kind == "turn":
                    act.wait_ge(prob_turned, i + 1)
                    if i >= 2:
                        act.wait_ge(head_done, i - 1)
                    nc.scalar.activation(mpT(i), ps[:, 7, 0:384], ACT.Copy).then_inc(probT_ready, 1)

            act.wait_ge(hg_done, 1)
            act.wait_ge(level_done, 2 * NLEV)
            nc.scalar.activation(squares[:, 0:1024], banks(2, 4).rearrange("p b n -> p (b n)"),
                                 ACT.Square).then_inc(hg_squared, 1)
            act.wait_ge(hg_summed, 1)
            nc.scalar.activation(hg_rstd[:, :], hg_ssq[:, :], ACT.Sqrt, bias=eps[:, :],
                                 scale=1.0 / HD).then_inc(hg_std, 1)

            act.wait_ge(residual_ready, 1)
            norm_stats(2, h, hn)
            for n, g in enumerate((X_Q0, X_Q1)):
                dst = qxT[:, 4 * n:4 * n + 4, :].rearrange("p c t -> p (c t)")
                keep_group(g, 2 * n, dst).then_inc(group_kept, 1)
            for i in range(XH + 1):
                if i < XH:
                    act.wait_ge(xs_max, i + 1)
                    if i >= 2:
                        act.wait_ge(xp_turned, i - 1)
                    for t in range(TT):
                        nc.scalar.activation(xp(i)[:, t, :], ps[:, i % 2, t * T:(t + 1) * T], ACT.Exp,
                                             bias=nmx[:, i % 2, t:t + 1], scale=XHD ** -0.5,
                                             accum_out=psum_row[:, i % 2, t:t + 1]).then_inc(xs_prob, 1)
                if i >= 1:
                    n = i - 1
                    act.wait_ge(xp_turned, n + 1)
                    if n >= 1:
                        act.wait_ge(xo_done, n)
                    nc.scalar.activation(xpT.rearrange("p k q -> p (k q)"), ps[:, 4, :],
                                         ACT.Copy).then_inc(xpT_ready, 1)
            act.wait_ge(residual_ready, 2)
            norm_stats(3, h, hn)
            act.wait_ge(hn_ready, 8)
            act.wait_ge(group_done, C_O1 + 1)
            nc.scalar.activation(xn_part[0], hn[:, :, :], ACT.Copy).then_inc(parts_ready, 1)
            act.wait_ge(router_max, 2)
            for t in range(TT):
                nc.scalar.activation(elog[:, t, :], logits[:, t, :], ACT.Exp,
                                     bias=ntop[:, t:t + 1]).then_inc(router_exp, 1)
            act.wait_ge(parts_ready, 2)
            nc.scalar.activation(xn_part[1], hn[:, :, :], ACT.Copy).then_inc(parts_ready, 1)

            def keep_sgT(done):
                for n in range(2):
                    last = nc.scalar.activation(sgT[64 * n:64 * n + 64, n, :], ps[64 * n:64 * n + 64, 7, 0:T],
                                                ACT.Copy)
                last.then_inc(done, 1)

            act.wait_ge(loop_zeroed, 7)
            act.wait_ge(table_ready, 1)
            act.sem_inc(actT_ready, 1)
            with act.Fori(0, NE) as e:
                count = act.value_load(tab[0:1, 0, bass.ds(e, 1)], min_val=0, max_val=T)
                with act.If(count > SLOTS):
                    first = act.value_load(tab[0:1, 1, bass.ds(e, 1)], min_val=0, max_val=NE)
                    with act.Fori(1, MAXBLK) as q:
                        with act.If(count > q * SLOTS):
                            n = first + q
                            act.wait_ge(m_turned, n)
                            act.wait_ge(scattered, e + 1)
                            keep_sgT(m_sgT)
                            act.wait_ge(m_glu, n)
                            nc.scalar.activation(sig, glu, ACT.Sigmoid, scale=ALPHA).then_inc(m_sig, 1)
                            act.wait_ge(m_actturn, n)
                            nc.scalar.activation(actT.rearrange("p q j s -> p (q j s)"), ps[:, 7, :],
                                                 ACT.Copy).then_inc(m_actT, 1)
                            act.wait_ge(m_scattered, n)
                            act.sem_inc(m_closed, 1)
                act.wait_ge(glu_ready, e + 1)
                nc.scalar.activation(sig, glu, ACT.Sigmoid, scale=ALPHA).then_inc(sig_ready, 1)
                act.wait_ge(pickg_turned, e + 2)
                act.wait_ge(scattered, e + 1)
                keep_sgT(sgT_ready)
                act.wait_ge(act_turned, e + 2)
                nc.scalar.activation(actT.rearrange("p q j s -> p (q j s)"), ps[:, 7, :],
                                     ACT.Copy).then_inc(actT_ready, 1)
            act.wait_ge(residual_ready, 3)
            norm_stats(4, h, hn)

        @block.vector
        def _(dve):
            link = linker(dve, dve_chain)

            def norm_rows(n, src, dst):
                dve.wait_ge(std_ready, n + 1)
                link(nc.vector.reciprocal(rstd[:, :], std[:, :]))
                for t in range(TT):
                    nc.vector.tensor_scalar(dst[:, t, :], src[:, t, :], rstd[:, t:t + 1], None,
                                            ALU.mult).then_inc(hn_ready, 1)

            def norm_gain(n, dst):
                for half in range(2):
                    dve.wait_ge(hn_turned, 2 * n + half + 1)
                    g = gains[:, n, 4 * half:4 * half + 4].unsqueeze(2).to_broadcast([P, 4, T])
                    src = banks(4 + 2 * half, 6 + 2 * half).rearrange("p b (c t) -> p (b c) t", c=2)
                    nc.vector.tensor_tensor(dst[:, 4 * half:4 * half + 4, :], src, g,
                                            ALU.mult).then_inc(hnT_ready, 1)

            norm_rows(0, h, hn)
            dve.wait_ge(small_loaded, 16 * 7)
            norm_gain(0, hnT)
            norm_rows(1, mem_sb, mem_n)
            link(nc.vector.tensor_tensor(lb[:, 4, :], lbl[:, 0, :], lbl[:, 1, :], ALU.max))
            for r in range(2):
                ins = nc.vector.tensor_tensor(lb[:, r, :], lbl[:, r, :], lb[:, 4, :], ALU.subtract)
                if r == 0:
                    link(ins)
            ins.then_inc(lb_exp, 1)
            dve.wait_ge(masks_ready, 7)
            link(nc.vector.tensor_tensor(iota_i[:, 0, :], iota_i[:, 0, :], iota_i[:, 1, :], ALU.bitwise_xor))
            link(nc.vector.tensor_copy(xor_f[:, :], iota_i[:, 0, :]))
            link(nc.vector.tensor_tensor(xor_f[:, :], xor_f[:, :], before[:, :], ALU.mult))
            for l, m in enumerate(LEVELS):
                link(nc.vector.tensor_scalar(factor[0][:, 0:P], xor_f[:, :], float(m), None, ALU.is_ge))
                link(nc.vector.scalar_tensor_tensor(out=lmask[:, l, :], in0=xor_f[:, :], scalar=float(2 * m),
                                                    in1=factor[0][:, 0:P], op0=ALU.is_lt, op1=ALU.mult))
            link(nc.vector.tensor_copy(lmask[:, 7, :], ident[:, :]))
            link(nc.vector.memset(a_in, 0.0))
            norm_gain(1, memT)
            dve.wait_ge(lb_exp, 2)
            link(nc.vector.tensor_tensor(lb[:, 4, :], lb[:, 2, :], lb[:, 3, :], ALU.add))
            link(nc.vector.reciprocal(lb[:, 5, :], lb[:, 4, :]))
            link(nc.vector.tensor_tensor(lb[:, 0, :], lb[:, 2, :], lb[:, 5, :], ALU.mult))
            link(nc.vector.tensor_scalar(lb[:, 1, :], lb[:, 0, :], -1.0, 1.0, ALU.mult, ALU.add))
            dve.wait_ge(group_kept, G_F + 1)
            link(nc.vector.tensor_scalar_add(fgate, fgate, 1.0))
            link(nc.vector.reciprocal(fgate, fgate))
            for c in range(NPAIR):
                cols = slice(c * T, (c + 1) * T)
                link(nc.vector.tensor_scalar(fgate[:, cols], fgate[:, cols], lb[:, 1, c:c + 1],
                                             lb[:, 0, c:c + 1], ALU.mult, ALU.add))
            dve.wait_ge(gate_ready, 1)
            link(nc.vector.tensor_scalar_add(tmp, tmp, 1.0))
            link(nc.vector.reciprocal(tmp, tmp))
            link(nc.vector.tensor_tensor(gq, gq, tmp, ALU.mult))
            nc.vector.tensor_scalar(kgate, fgate, -1.0, 1.0, ALU.mult, ALU.add).then_inc(log_ready, 1)
            link(nc.vector.memset(factor[1], 1.0))
            link(nc.vector.memset(factor[1].rearrange("p (n m) -> p n m", m=P)[:, :, 0:1], 0.0))
            dve.wait_ge(log_ready, 2)
            link(nc.vector.tensor_tensor_scan(bsum, factor[1], tmp, 0.0, ALU.mult, ALU.add))

            def differences(l):
                m = P if l == OFF else LEVELS[l]
                b1st, b2nd = blocks_of(bsum, m)
                f1st, f2nd = blocks_of(factor[l % 2], m)
                if l >= 2:
                    dve.wait_ge(pad_ready, 2 * (l - 1))
                    dve.wait_ge(level_done, 2 * (l - 1))
                mid = b1st[:, :, m - 1:m].to_broadcast([P, 1024 // (2 * m), m])
                if l == OFF:
                    link(nc.vector.tensor_copy(f2nd, b2nd))
                else:
                    link(nc.vector.tensor_tensor(f2nd, b2nd, mid, ALU.subtract))
                nc.vector.tensor_tensor(f1st, mid, b1st, ALU.subtract).then_inc(diff_ready, 1)

            differences(0)
            for item in order:
                kind, i = item[0], item[1]
                if kind == "proj" and i == G_G and item[2] == 3:
                    dve.wait_ge(gate_ready, 2)
                    link(nc.vector.tensor_scalar_add(tmp, tmp, 1.0))
                    link(nc.vector.reciprocal(tmp, tmp))
                    link(nc.vector.tensor_tensor(sgate, sgate, tmp, ALU.mult))
                elif kind == "decay":
                    if i + 1 <= OFF:
                        differences(i + 1)
                    if i <= OFF:
                        dve.wait_ge(decay_ready, i + 1)
                        m = P if i == OFF else LEVELS[i]
                        f1st, f2nd = blocks_of(factor[i % 2], m)
                        link(nc.vector.tensor_tensor(f2nd, f2nd, blocks_of(gq, m)[1], ALU.mult))
                        nc.vector.tensor_tensor(f1st, f1st, blocks_of(kgate, m)[0], ALU.mult).then_inc(factor_ready, 1)
                elif kind == "level":
                    if i == OFF:
                        dve.wait_ge(level_done, 2 * i + 2)
                        nc.vector.tensor_copy(a_off, banks(2, 4).rearrange("p b n -> p (b n)")).then_inc(level_kept, 2)
                        continue
                    mask = lmask[:, 7 if i == DIAG else i, :].unsqueeze(1).to_broadcast([P, 2, P])
                    for half in range(2):
                        dve.wait_ge(level_done, 2 * i + half + 1)
                        for c in range(NPAIR):
                            ins = nc.vector.copy_predicated(
                                a_in.rearrange("p (c n j t) -> p c n j t", c=NPAIR, n=2, j=2)[:, c, half],
                                mask,
                                banks(2 + 2 * half, 4 + 2 * half).rearrange(
                                    "p b (c j t) -> p (b c) j t", c=2, j=2)[:, c])
                            if c < NPAIR - 1:
                                link(ins)
                        ins.then_inc(level_kept, 1)
                        dve.wait_ge(level_kept, 2 * i + half + 1)
                elif kind == "score":
                    dve.wait_ge(score_done, i + 1)
                    if i >= 2:
                        dve.wait_ge(prob_turned, i - 1)
                    for t in range(TT):
                        cols = slice(0, 128) if t == 0 else slice(128, 384)
                        link(nc.vector.tensor_tensor_reduce(
                            out=mp(i)[:, cols], in0=ps[:, 6, cols],
                            in1=cmask[:, :, :].rearrange("p a b -> p (a b)")[:, cols],
                            scale=HD ** -0.5, scalar=MASKED, op0=ALU.add, op1=ALU.max,
                            accum_out=mx[:, i % 2, t:t + 1]))
                    nc.vector.tensor_scalar(nmx[:, i % 2, :], mx[:, i % 2, :], -1.0, None,
                                            ALU.mult).then_inc(score_kept, 1)
                elif kind == "turn":
                    dve.wait_ge(prob_ready, 2 * i + 2)
                    if i >= 2:
                        dve.wait_ge(head_kept, i - 1)
                    nc.vector.reciprocal(rinv[:, i % 2, :], psum_row[:, i % 2, :]).then_inc(rinv_ready, 1)
                elif kind == "out":
                    dve.wait_ge(rinv_ready, i + 1)
                    dve.wait_ge(head_done, i + 1)
                    for t in range(TT):
                        ins = nc.vector.tensor_scalar(mix[:, t, i * HD:(i + 1) * HD],
                                                      ps[:, 7, 384 + t * HD:384 + (t + 1) * HD],
                                                      rinv[:, i % 2, t:t + 1], None, ALU.mult)
                        if t == 0:
                            link(ins)
                    ins.then_inc(head_kept, 1)

            dve.wait_ge(mix_turned, 1)
            nc.vector.tensor_copy(mixT[:, 0:4, :], banks(4, 6).rearrange("p b (c t) -> p (b c) t", c=2)).then_inc(mixT_ready, 1)
            dve.wait_ge(hg_squared, 1)
            nc.vector.tensor_reduce(hg_ssq[:, :], squares[:, 0:1024].rearrange("p (n d) -> p n d", d=HD),
                                    axis=AX_X, op=ALU.add).then_inc(hg_summed, 1)
            dve.wait_ge(hg_std, 1)
            link(nc.vector.reciprocal(hg_rstd[:, :], hg_rstd[:, :]))
            o_heads = banks(2, 4).rearrange("p b (n d) -> p (b n) d", d=HD)
            m_heads = squares[:, 1024:2048].rearrange("p (n d) -> p n d", d=HD)
            link(nc.vector.tensor_tensor(m_heads, o_heads,
                                         hg_rstd[:, :].unsqueeze(2).to_broadcast([P, 2 * NH, HD]), ALU.mult))
            nc.vector.tensor_tensor(mix[:, :, 512:1024], squares[:, 1024:2048].rearrange("p (t d) -> p t d", t=TT),
                                    sgate.rearrange("p (t d) -> p t d", t=TT), ALU.mult).then_inc(hg_mix_ready, 1)
            dve.wait_ge(mix_turned, 2)
            nc.vector.tensor_tensor(mixT[:, 4:8, :], banks(4, 6).rearrange("p b (c t) -> p (b c) t", c=2),
                                    hg_gain[:, :].unsqueeze(2).to_broadcast([P, NPAIR, T]),
                                    ALU.mult).then_inc(mixT_ready, 1)

            def add_residual(first_group, bank_of):
                for n in range(2):
                    dve.wait_ge(group_done, first_group + n + 1)
                    ins = nc.vector.tensor_tensor(h[:, :, n * GW:(n + 1) * GW], banks(bank_of[n], bank_of[n] + 2),
                                                  h[:, :, n * GW:(n + 1) * GW], ALU.add)
                    if n == 0:
                        link(ins)
                ins.then_inc(residual_ready, 1)

            add_residual(W_O0, (0, 6))
            norm_rows(2, h, hn)
            norm_gain(2, hnT)
            for i in range(XH + 2):
                if i < XH:
                    dve.wait_ge(xs_done, i + 1)
                    if i >= 2:
                        dve.wait_ge(xs_prob, 2 * (i - 1))
                    link(nc.vector.tensor_reduce(mx[:, i % 2, :], ps[:, i % 2, :].rearrange("p (t k) -> p t k", t=TT),
                                                 axis=AX_X, op=ALU.max))
                    nc.vector.tensor_scalar(nmx[:, i % 2, :], mx[:, i % 2, :], -XHD ** -0.5, None,
                                            ALU.mult).then_inc(xs_max, 1)
                if 1 <= i <= XH:
                    n = i - 1
                    dve.wait_ge(xs_prob, 2 * i)
                    link(nc.vector.reciprocal(rinv[:, n % 2, :], psum_row[:, n % 2, :]))
                    for t in range(TT):
                        nc.vector.tensor_scalar(xp(n)[:, t, :], xp(n)[:, t, :], rinv[:, n % 2, t:t + 1], None,
                                                ALU.mult).then_inc(xs_scaled, 1)
                if i >= 2:
                    n = i - 2
                    dve.wait_ge(xo_done, n + 1)
                    nc.vector.tensor_copy(qxT[:, 2 * n:2 * n + 2, :],
                                          ps[:, 5, :].rearrange("p (c q) -> p c q", c=2)).then_inc(xo_kept, 1)
            add_residual(C_O0, (6, 2))
            norm_rows(3, h, hn)
            norm_gain(3, hnT)

            dve.wait_ge(parts_ready, 1)
            nc.vector.tensor_tensor(hn[:, :, :], hn[:, :, :], xn_part[0], ALU.subtract).then_inc(parts_ready, 1)
            dve.wait_ge(router_done, 1)
            dve.wait_ge(router_loaded, 32)
            for t in range(TT):
                link(nc.vector.tensor_tensor(logits[:, t, :], ps[:, 4, t * NE:(t + 1) * NE], br[:, :], ALU.add))
                link(nc.vector.max(top8[:, t, :], logits[:, t, :]))
                nc.vector.tensor_scalar(ntop[:, t:t + 1], top8[:, t, 0:1], -1.0, None, ALU.mult).then_inc(router_max, 1)
                link(nc.vector.max_index(idx8[:, t, :], top8[:, t, :], logits[:, t, :]))
                link(nc.vector.tensor_copy(idx8f[:, t, :], idx8[:, t, :]))
                link(nc.vector.tensor_scalar(sel[:, t, :], iota_s[:, 0:NE], idx8f[:, t, 0:1], None, ALU.is_equal))
                for j in range(1, TOPK):
                    ins = nc.vector.scalar_tensor_tensor(out=sel[:, t, :], in0=iota_s[:, 0:NE],
                                                         scalar=idx8f[:, t, j:j + 1], in1=sel[:, t, :],
                                                         op0=ALU.is_equal, op1=ALU.add)
                    if j < TOPK - 1:
                        link(ins)
                ins.then_inc(chosen, 1)
            dve.wait_ge(router_exp, 2)
            dve.wait_ge(chosen, 2)
            dve.wait_ge(loop_zeroed, 7)
            for t in range(TT):
                link(nc.vector.tensor_tensor_reduce(out=elog[:, t, :], in0=elog[:, t, :], in1=sel[:, t, :],
                                                    scale=1.0, scalar=0.0, op0=ALU.mult, op1=ALU.add,
                                                    accum_out=gate_sum[:, t:t + 1]))
                link(nc.vector.reciprocal(gate_sum[:, t:t + 1], gate_sum[:, t:t + 1]))
                nc.vector.tensor_scalar(gates[:, t, 0:NE], elog[:, t, :], gate_sum[:, t:t + 1], None,
                                        ALU.mult).then_inc(chosen, 1)
            dve.wait_ge(chosen, 4)
            dve.wait_ge(ranked, 1)
            for t in range(TT):
                link(nc.vector.scalar_tensor_tensor(out=posm[:, t, 0:NE], in0=ps[:, 5, t * NE:(t + 1) * NE],
                                                    scalar=1.0, in1=sel[:, t, :], op0=ALU.add, op1=ALU.mult))
                link(nc.vector.tensor_scalar_add(posm[:, t, 0:NE], posm[:, t, 0:NE], -1.0))
            cnt = tabf[0:1, 0, :]
            link(nc.vector.tensor_copy(cnt, ps[0:1, 5, 2 * NE:3 * NE]))
            link(nc.vector.tensor_scalar(tabf[0:1, 1, :], cnt, float(SLOTS), None, ALU.is_gt))
            for q in range(2, MAXBLK):
                link(nc.vector.scalar_tensor_tensor(out=tabf[0:1, 1, :], in0=cnt, scalar=float(q * SLOTS),
                                                    in1=tabf[0:1, 1, :], op0=ALU.is_gt, op1=ALU.add))
            link(nc.vector.memset(tabf[0:1, 2, :], 1.0))
            link(nc.vector.tensor_tensor_scan(tabf[0:1, 3, :], tabf[0:1, 2, :], tabf[0:1, 1, :], 0.0,
                                              ALU.mult, ALU.add))
            link(nc.vector.tensor_tensor(tabf[0:1, 4, :], tabf[0:1, 3, :], tabf[0:1, 1, :], ALU.subtract))
            link(nc.vector.tensor_copy(tab[0:1, 0, :], cnt))
            nc.vector.tensor_copy(tab[0:1, 1, :], tabf[0:1, 4, :]).then_inc(table_ready, 1)
            dve.wait_ge(gates_turned, 1)
            nc.vector.tensor_copy(gatesT.rearrange("p t s -> p (t s)"), ps[:, 4, 0:T]).then_inc(gatesT_ready, 1)
            dve.wait_ge(parts_ready, 3)
            nc.vector.tensor_tensor(xn_part[2], hn[:, :, :], xn_part[1], ALU.subtract).then_inc(parts_ready, 1)

            moe_gain = gains[:, 3, :].unsqueeze(2).to_broadcast([P, KC, SLOTS])

            def one_hot(e, slots, done):
                for t in range(TT):
                    last = nc.vector.tensor_scalar(pick[:, t, :], slots, posm[:, t, bass.ds(e, 1)], None,
                                                   ALU.is_equal)
                last.then_inc(done, 1)

            def one_hot_gated(e, slots, done):
                for t in range(TT):
                    for n in range(2):
                        last = nc.vector.tensor_scalar(pick_gated[:, t, n, :], slots, posm[:, t, bass.ds(e, 1)],
                                                       gates[:, t, bass.ds(e, 1)], ALU.is_equal, ALU.mult)
                last.then_inc(done, 1)

            def keep_gathered(dst, done):
                nc.vector.tensor_tensor(dst, ps[:, 6, :].rearrange("p (c s) -> p c s", c=KC), moe_gain,
                                        ALU.mult).then_inc(done, 1)

            h_pair = banks(4, 6).rearrange("p b (n two) -> p b n two", two=2)

            def as_banks(ap):
                return ap.rearrange("p (b n) -> p b n", b=2)

            one_hot(0, iota_s[:, 0:SLOTS], pick_ready)
            nc.vector.tensor_copy(b1_pick, ident[:, 0:1].to_broadcast([P, SLOTS])).then_inc(b1_pick_ready, 1)
            dve.wait_ge(gathered, 1)
            keep_gathered(xgT, xgT_ready)

            dve.wait_ge(table_ready, 1)
            for free in (act_ready, y_ready):
                dve.sem_inc(free, 1)
            with dve.Fori(0, NE) as e:
                count = dve.value_load(tab[0:1, 0, bass.ds(e, 1)], min_val=0, max_val=T)
                with dve.If(count > SLOTS):
                    first = dve.value_load(tab[0:1, 1, bass.ds(e, 1)], min_val=0, max_val=NE)
                    with dve.Fori(1, MAXBLK) as q:
                        with dve.If(count > q * SLOTS):
                            n = first + q
                            slots = iota_s[:, bass.ds(q * SLOTS, SLOTS)]
                            dve.wait_ge(gathered, e + 1)
                            one_hot(e, slots, m_pick)
                            dve.wait_ge(pickg_turned, e + 1)
                            one_hot_gated(e, slots, m_pick)
                            dve.wait_ge(m_gathered, n)
                            keep_gathered(xgT_more, m_xgT)
                            dve.wait_ge(m_up, n)
                            nc.vector.tensor_scalar_min(as_banks(glu), h_pair[:, :, :, 0], LIMIT).then_inc(m_glu, 1)
                            nc.vector.tensor_scalar(as_banks(lin), h_pair[:, :, :, 1], LIMIT, -LIMIT, ALU.min,
                                                    ALU.max).then_inc(m_dve, 1)
                            dve.wait_ge(m_sig, n)
                            dve.wait_ge(m_dve, n * 2 - 1)
                            nc.vector.scalar_tensor_tensor(out=lin, in0=lin, scalar=1.0, in1=sig, op0=ALU.add,
                                                           op1=ALU.mult).then_inc(m_dve, 1)
                            dve.wait_ge(m_dve, n * 2)
                            dve.wait_ge(m_glu, n)
                            dve.wait_ge(act_turned, e + 1)
                            nc.vector.tensor_tensor(actb, lin, glu, ALU.mult).then_inc(m_act, 1)
                            dve.wait_ge(m_down, n)
                            dve.wait_ge(scattered, e + 1)
                            nc.vector.tensor_copy(y_sb, ps[:, 6, :]).then_inc(m_y, 1)
                            dve.wait_ge(m_scattered, n)
                            dve.sem_inc(m_closed, 1)
                dve.wait_ge(pickg_turned, e + 1)
                one_hot_gated(e, iota_s[:, 0:SLOTS], pickg_ready)
                dve.wait_ge(gathered, e + 1)
                one_hot(e + 1, iota_s[:, 0:SLOTS], pick_ready)
                dve.wait_ge(bias_added, e + 1)
                nc.vector.tensor_copy(b1_pick, ident[:, bass.ds(e + 1, 1)].to_broadcast([P, SLOTS])).then_inc(
                    b1_pick_ready, 1)
                dve.wait_ge(up_done, e + 1)
                nc.vector.tensor_scalar_min(as_banks(glu), h_pair[:, :, :, 0], LIMIT).then_inc(glu_ready, 1)
                nc.vector.tensor_scalar(as_banks(lin), h_pair[:, :, :, 1], LIMIT, -LIMIT, ALU.min,
                                        ALU.max).then_inc(dve_loop, 1)
                dve.wait_ge(sig_ready, e + 1)
                dve.wait_ge(dve_loop, e * 2 + 1)
                nc.vector.scalar_tensor_tensor(out=lin, in0=lin, scalar=1.0, in1=sig, op0=ALU.add,
                                               op1=ALU.mult).then_inc(dve_loop, 1)
                dve.wait_ge(dve_loop, e * 2 + 2)
                dve.wait_ge(glu_ready, e + 1)
                dve.wait_ge(act_turned, e + 1)
                nc.vector.tensor_tensor(actb, lin, glu, ALU.mult).then_inc(act_ready, 1)
                dve.wait_ge(gathered, e + 2)
                keep_gathered(xgT, xgT_ready)
                dve.wait_ge(down_done, e + 1)
                dve.wait_ge(scattered, e + 1)
                nc.vector.tensor_copy(y_sb, ps[:, 6, :]).then_inc(y_ready, 1)

            dve.wait_ge(scattered, NE + 1)
            nc.vector.tensor_tensor(h[:, :, :].rearrange("p t (n d) -> p (t n) d", n=2), banks(0, 4),
                                    h[:, :, :].rearrange("p t (n d) -> p (t n) d", n=2),
                                    ALU.add).then_inc(residual_ready, 1)
            norm_rows(4, h, hn)
            dve.wait_ge(lnf_loaded, 16)
            dve.wait_ge(hn_ready, 10)
            nc.vector.tensor_tensor(res, hn[:, :, :], lnf.unsqueeze(1).to_broadcast([P, TT, D]),
                                    ALU.mult).then_inc(hnT_ready, 1)

        @block.tensor
        def _(pe):
            def turn_rows(n, src):
                for half in range(2):
                    pe.wait_ge(hn_ready, 2 * n + 2)
                    for c in range(4 * half, 4 * half + 4):
                        for t in range(TT):
                            col = (c % 2) * T + t * P
                            last = nc.tensor.transpose(ps[:, 4 + c // 2, col:col + P], src[:, t, c * P:(c + 1) * P],
                                                       ident[:, :])
                    last.then_inc(hn_turned, 1)

            def feature_quarter(g, m, bank, srcT):
                for k in range(KC):
                    last = nc.tensor.matmul(ps[:, bank + m // 2, (m % 2) * T:(m % 2 + 1) * T],
                                            group_unit(g, k)[:, m * P:(m + 1) * P], srcT[:, k, :],
                                            start=(k == 0), stop=(k == KC - 1))
                return last

            def token_quarter(g, j, bank, srcT, bank_step=1):
                t = j // 2
                for k in range(4 * (j % 2), 4 * (j % 2) + 4):
                    last = nc.tensor.matmul(ps[:, bank + t * bank_step, :], srcT[:, k, t * P:(t + 1) * P],
                                            group_unit(g, k), start=(k == 0), stop=(k == KC - 1))
                return last

            def group_start(g):
                group_arrived(pe, g, 0)
                group_arrived(pe, g, 1)

            def whole_group(g, bank, srcT):
                group_start(g)
                for m in range(4):
                    last = feature_quarter(g, m, bank, srcT)
                last.then_inc(group_done, 1)

            pe.wait_ge(consts_ready, 2)
            turn_rows(0, hn)
            pe.wait_ge(hnT_ready, 2)
            whole_group(G_F, 0, hnT)
            whole_group(G_Q, 2, hnT)
            turn_rows(1, mem_n)
            pe.wait_ge(group_kept, G_F + 1)
            whole_group(M_Q, 0, hnT)
            pe.wait_ge(group_kept, M_Q + 1)
            whole_group(M_K, 0, hnT)
            pe.wait_ge(hnT_ready, 4)

            for item in order:
                kind, i = item[0], item[1]
                if kind == "proj":
                    j = item[2]
                    if j == 0:
                        pe.wait_ge(group_kept, i)
                        group_start(i)
                    if i in FEATURE_GROUPS:
                        last = feature_quarter(i, j, 0, memT)
                    else:
                        last = token_quarter(i, j, 0, hnT if i <= G_G else memT)
                    if j == 3:
                        last.then_inc(group_done, 1)
                elif kind == "level":
                    pe.wait_ge(pad_ready, 2 * i + 2)
                    if i >= 1:
                        pe.wait_ge(level_kept, 2 * i)
                    stationary = (kgate if i == DIAG else factor[i % 2]).rearrange("p (c t) -> p c t", c=NPAIR)
                    for half in range(1 if i == OFF else 2):
                        for c in range(NPAIR):
                            s0 = half * P
                            t0 = P if i == OFF else s0
                            last = nc.tensor.matmul(
                                ps[:, 2 + 2 * half + c // 2, (c % 2) * T:(c % 2 + 1) * T],
                                stationary[:, c, s0:s0 + P], factor_pad[:, c, :, t0:t0 + P],
                                start=True, stop=True)
                        last.then_inc(level_done, 2 if i == OFF else 1)
                elif kind == "score":
                    if i == 0:
                        pe.wait_ge(group_kept, M_K + 1)
                    else:
                        pe.wait_ge(score_kept, i)
                    rows = slice(64 * (i % 2), 64 * (i % 2) + 64)
                    nc.tensor.matmul(ps[:, 6, 0:128], mqT[rows, i // 2, 0:P], mkT[rows, i // 2, 0:P],
                                     start=True, stop=True)
                    nc.tensor.matmul(ps[:, 6, 128:384], mqT[rows, i // 2, P:T], mkT[rows, i // 2, :],
                                     start=True, stop=True).then_inc(score_done, 1)
                elif kind == "turn":
                    pe.wait_ge(prob_ready, 2 * i + 2)
                    if i >= 1:
                        pe.wait_ge(head_kept, i)
                    for c in range(3):
                        last = nc.tensor.transpose(ps[:, 7, c * P:(c + 1) * P], mp(i)[:, c * P:(c + 1) * P], ident[:, :])
                    last.then_inc(prob_turned, 1)
                elif kind == "out":
                    pe.wait_ge(group_kept, M_V + 1)
                    pe.wait_ge(probT_ready, i + 1)
                    cols = slice(i * HD, (i + 1) * HD)
                    nc.tensor.matmul(ps[:, 7, 384:448], mpT(i)[:, 0:P], mv[:, 0, cols], start=True, stop=True)
                    nc.tensor.matmul(ps[:, 7, 448:512], mpT(i)[:, P:2 * P], mv[:, 0, cols], start=True, stop=False)
                    nc.tensor.matmul(ps[:, 7, 448:512], mpT(i)[:, 2 * P:3 * P], mv[:, 1, cols], start=False,
                                     stop=True).then_inc(head_done, 1)

            pe.wait_ge(level_kept, 2 * NLEV)
            a5 = a_in.rearrange("p (c n j t) -> p c n j t", c=NPAIR, n=2, j=2)
            o4 = a_off.rearrange("p (c j t) -> p c j t", c=NPAIR, j=2)
            for i in range(NH):
                c, j, cols = i // 2, i % 2, slice(i * HD, (i + 1) * HD)
                nc.tensor.matmul(ps[:, 2, cols], a5[:, c, 0, j, :], gi[:, 0, cols], start=True, stop=True)
                nc.tensor.matmul(ps[:, 3, cols], a5[:, c, 1, j, :], gi[:, 1, cols], start=True, stop=False)
                last = nc.tensor.matmul(ps[:, 3, cols], o4[:, c, j, :], gi[:, 0, cols], start=False, stop=True)
            last.then_inc(hg_done, 1)

            def turn_mix(half):
                for c in range(4 * half, 4 * half + 4):
                    for t in range(TT):
                        col = (c % 2) * T + t * P
                        last = nc.tensor.transpose(ps[:, 4 + c // 2 - 2 * half, col:col + P],
                                                   mix[:, t, c * P:(c + 1) * P], ident[:, :])
                last.then_inc(mix_turned, 1)

            pe.wait_ge(head_kept, NH)
            pe.wait_ge(group_kept, X_V1 + 1)
            turn_mix(0)
            pe.wait_ge(mixT_ready, 1)
            group_start(W_O0)
            group_start(W_O1)
            for half in range(2):
                if half == 1:
                    pe.wait_ge(hg_mix_ready, 1)
                    turn_mix(1)
                    pe.wait_ge(mixT_ready, 2)
                for n, g in enumerate((W_O0, W_O1)):
                    token_quarter(g, half, 6 * n, mixT)
                    last = token_quarter(g, 2 + half, 6 * n, mixT)
                    if half == 1:
                        last.then_inc(group_done, 1)

            turn_rows(2, hn)
            pe.wait_ge(hnT_ready, 6)
            whole_group(X_Q0, 0, hnT)
            whole_group(X_Q1, 2, hnT)
            pe.wait_ge(group_kept, X_V1 + 2)
            group_start(C_O0)
            group_start(C_O1)
            for i in range(XH + 3):
                if i < XH:
                    if i == 2:
                        pe.wait_ge(group_kept, X_V1 + 3)
                    if i >= 2:
                        pe.wait_ge(xs_prob, 2 * (i - 1))
                    for t in range(TT):
                        for c in range(2):
                            last = nc.tensor.matmul(ps[:, i % 2, t * T:(t + 1) * T],
                                                    qxT[:, 2 * i + c, t * P:(t + 1) * P], KxT[:, 2 * i + c, :],
                                                    start=(c == 0), stop=(c == 1))
                    last.then_inc(xs_done, 1)
                if i >= 3:
                    n = i - 3
                    pe.wait_ge(xo_kept, n + 1)
                    for q, g in enumerate((C_O0, C_O1)):
                        for t in range(TT):
                            for k in (2 * n, 2 * n + 1):
                                last = nc.tensor.matmul(ps[:, (6, 2)[q] + t, :], qxT[:, k, t * P:(t + 1) * P],
                                                        group_unit(g, k), start=(k == 0), stop=(k == KC - 1))
                        if n == XH - 1:
                            last.then_inc(group_done, 1)
                if 1 <= i <= XH:
                    n = i - 1
                    pe.wait_ge(xs_scaled, 2 * n + 2)
                    if n >= 1:
                        pe.wait_ge(xpT_ready, n)
                    for t in range(TT):
                        for k in range(TT):
                            last = nc.tensor.transpose(ps[:, 4, k * T + t * P:k * T + (t + 1) * P],
                                                       xp(n)[:, t, k * P:(k + 1) * P], ident[:, :])
                    last.then_inc(xp_turned, 1)
                if 1 <= i <= XH:
                    n = i - 1
                    pe.wait_ge(xpT_ready, n + 1)
                    if n >= 1:
                        pe.wait_ge(xo_kept, n)
                    for c in range(2):
                        for k in range(TT):
                            last = nc.tensor.matmul(ps[:, 5, c * T:(c + 1) * T],
                                                    Vx[:, k, (2 * n + c) * P:(2 * n + c + 1) * P], xpT[:, k, :],
                                                    start=(k == 0), stop=(k == 1))
                    last.then_inc(xo_done, 1)

            turn_rows(3, hn)
            pe.wait_ge(hnT_ready, 8)
            pe.wait_ge(router_loaded, 32)
            for t in range(TT):
                for k in range(KC):
                    last = nc.tensor.matmul(ps[:, 4, t * NE:(t + 1) * NE], hnT[:, k, t * P:(t + 1) * P], wr[:, k, :],
                                            start=(k == 0), stop=(k == KC - 1))
            last.then_inc(router_done, 1)
            pe.wait_ge(chosen, 2)
            pe.wait_ge(masks_ready, 7)
            nc.tensor.matmul(ps[:, 5, 0:NE], before[:, :], sel[:, 0, :], start=True, stop=True)
            nc.tensor.matmul(ps[:, 5, NE:2 * NE], ones[:, :], sel[:, 0, :], start=True, stop=False)
            nc.tensor.matmul(ps[:, 5, NE:2 * NE], before[:, :], sel[:, 1, :], start=False, stop=True)
            nc.tensor.matmul(ps[:, 5, 2 * NE:3 * NE], ones[:, :], sel[:, 0, :], start=True, stop=False)
            nc.tensor.matmul(ps[:, 5, 2 * NE:3 * NE], ones[:, :], sel[:, 1, :], start=False,
                             stop=True).then_inc(ranked, 1)
            pe.wait_ge(chosen, 4)
            for t in range(TT):
                last = nc.tensor.transpose(ps[:, 4, t * P:(t + 1) * P], gates[:, t, :], ident[:, :])
            last.then_inc(gates_turned, 1)
            pe.wait_ge(gatesT_ready, 1)
            pe.wait_ge(loop_zeroed, 7)
            pe.wait_ge(bias_loaded, 32)
            for t in range(TT):
                for n in range(2):
                    nc.tensor.matmul(ps[:, 2 * t + n, :], gatesT[:, t, :], b2_sb[:, n * GW:(n + 1) * GW],
                                     start=True, stop=False, skip_group_check=True)

            def gather(done):
                for c in range(KC):
                    n = 0
                    for part in xn_part:
                        for t in range(TT):
                            last = nc.tensor.matmul(ps[:, 6, c * SLOTS:(c + 1) * SLOTS],
                                                    part[:, t, c * P:(c + 1) * P], pick[:, t, :],
                                                    start=(n == 0), stop=(n == 5))
                            n += 1
                last.then_inc(done, 1)

            def turn_gated(done):
                for t in range(TT):
                    last = nc.tensor.transpose(ps[:, 7, t * P:(t + 1) * P],
                                               pick_gated[:, t, :, :].rearrange("p n s -> p (n s)"), ident[:, :])
                last.then_inc(done, 1)

            def bias_up():
                for c in range(2):
                    for j in range(2):
                        last = nc.tensor.matmul(ps[64 * j:64 * j + 64, 4 + c, :], b1_pick,
                                                b1_sb[:, j * 1024 + c * GW:j * 1024 + (c + 1) * GW],
                                                start=True, stop=False)
                return last

            def up_unit(src, k):
                for c in range(2):
                    for j in range(2):
                        last = nc.tensor.matmul(ps[64 * j:64 * j + 64, 4 + c, :], src[:, k, :],
                                                expert_ring[:, k, j * 1024 + c * GW:j * 1024 + (c + 1) * GW],
                                                start=False, stop=(k == KC - 1))
                return last

            def turn_act(done):
                for q in range(4):
                    last = nc.tensor.transpose(ps[:, 7, q * P:(q + 1) * P], actb[:, q * P:(q + 1) * P], ident[:, :])
                last.then_inc(done, 1)

            def down_unit(v):
                for a in range(2):
                    kk = 2 * v + a
                    for n in range(2):
                        last = nc.tensor.matmul(ps[64 * n:64 * n + 64, 6, :], actT[:, kk % 4, kk // 4, :],
                                                expert_ring[:, 8 + v, a * D + n * GW:a * D + (n + 1) * GW],
                                                start=(kk == 0), stop=(kk == 7))
                return last

            def scatter(done):
                for t in range(TT):
                    for n in range(2):
                        last = nc.tensor.matmul(ps[:, 2 * t + n, :], sgT[:, n, t * P:(t + 1) * P], y_sb,
                                                start=False, stop=False, skip_group_check=True)
                last.then_inc(done, 1)

            pe.wait_ge(table_ready, 1)
            pe.wait_ge(parts_ready, 4)
            pe.wait_ge(pick_ready, 1)
            gather(gathered)
            for free in (pickg_turned, act_turned, scattered):
                pe.sem_inc(free, 1)
            with pe.Fori(0, NE) as e:
                count = pe.value_load(tab[0:1, 0, bass.ds(e, 1)], min_val=0, max_val=T)
                with pe.If(count > SLOTS):
                    first = pe.value_load(tab[0:1, 1, bass.ds(e, 1)], min_val=0, max_val=NE)
                    with pe.Fori(1, MAXBLK) as q:
                        with pe.If(count > q * SLOTS):
                            n = first + q
                            pe.wait_ge(m_pick, n * 2)
                            pe.wait_ge(xgT_ready, e + 1)
                            pe.wait_ge(y_ready, e + 1)
                            gather(m_gathered)
                            pe.wait_ge(actT_ready, e + 1)
                            turn_gated(m_turned)
                            pe.wait_ge(b1_pick_ready, e + 1)
                            pe.wait_ge(act_ready, e + 1)
                            bias_up()
                            pe.wait_ge(m_xgT, n)
                            for k in range(KC):
                                pe.wait_ge(expert_loaded[k], e * 16 + 16)
                                last = up_unit(xgT_more, k)
                            last.then_inc(m_up, 1)
                            pe.wait_ge(m_act, n)
                            pe.wait_ge(m_sgT, n)
                            turn_act(m_actturn)
                            pe.wait_ge(m_actT, n)
                            for v in range(4):
                                pe.wait_ge(expert_loaded[8 + v], e * 16 + 16)
                                last = down_unit(v)
                            last.then_inc(m_down, 1)
                            pe.wait_ge(m_y, n)
                            scatter(m_scattered)
                pe.wait_ge(b1_pick_ready, e + 1)
                pe.wait_ge(act_ready, e + 1)
                bias_up().then_inc(bias_added, 1)
                pe.wait_ge(xgT_ready, e + 1)
                for k in range(KC):
                    pe.wait_ge(expert_loaded[k], e * 16 + 16)
                    last = up_unit(xgT, k)
                    if k < KC - 1:
                        last.then_inc(unit_used, 1)
                last.then_inc(up_done, 1)
                pe.wait_ge(pick_ready, e + 2)
                pe.wait_ge(y_ready, e + 1)
                gather(gathered)
                pe.wait_ge(pickg_ready, e + 1)
                pe.wait_ge(actT_ready, e + 1)
                turn_gated(pickg_turned)
                pe.wait_ge(act_ready, e + 2)
                pe.wait_ge(sgT_ready, e + 1)
                turn_act(act_turned)
                pe.wait_ge(actT_ready, e + 2)
                pe.wait_ge(xgT_ready, e + 2)
                for v in range(4):
                    pe.wait_ge(expert_loaded[8 + v], e * 16 + 16)
                    last = down_unit(v)
                    if v < 3:
                        last.then_inc(unit_used, 1)
                last.then_inc(down_done, 1)
                pe.wait_ge(y_ready, e + 2)
                scatter(scattered)


_INS = ['x', 'mem', 'ln_mix_g', 'w_in', 'hgrn_lb_logits', 'hgrn_norm_g', 'w_out', 'ln_x_g', 'ln_mem_g', 'wq_x',
        'wkv_x', 'wo_x', 'ln_moe_g', 'w_router', 'b_router', 'w1', 'b1', 'w2', 'b2', 'ln_f_g']


def kernel(**inputs):
    import concourse.bacc as _bacc
    from concourse.bass_utils import run_bass_kernel_spmd as _run

    nc = _bacc.Bacc("TRN2", target_bir_lowering=False, num_devices=1)
    arrays, args = {}, []
    for name in _INS:
        a = np.ascontiguousarray(inputs[name])
        arrays[f"in_{name}_dram"] = a
        args.append(nc.dram_tensor(f"in_{name}_dram", a.shape, mybir.dt.from_np(a.dtype), kind="ExternalInput").ap())
    args.append(nc.dram_tensor("out_0_dram", (1, T, D), F32, kind="ExternalOutput").ap())
    build(nc, *args)
    r = _run(nc, [arrays], core_ids=[0])
    return r.results[0]["out_0_dram"]
```

```python
import numpy as np

import concourse.bass as bass
from concourse import mybir
from contextlib import ExitStack

F32 = mybir.dt.float32
BF16 = mybir.dt.bfloat16
I32 = mybir.dt.int32
U32 = mybir.dt.uint32
ALU = mybir.AluOpType
ACT = mybir.ActivationFunctionType
AX_X = mybir.AxisListType.X

P = 128
D = 1024
KC = D // P
T = 256
TT = T // P
HD = 64
NH = 8
NPAIR = NH // 2
GW = 512
XH, XHD = 4, 256
NE, TOPK = 32, 4
SLOTS = 64
MAXBLK = T // SLOTS
LIMIT, ALPHA = 7.0, 1.702
EPS = 1e-6
MASKED = -1e30
UNIT = 2048
EXPERT_UNITS = 12
FRONT_PAIRS = 3
LEVELS = [64, 32, 16, 8, 4, 2, 1]
TURN_BANKS = ((6, 4), (6, 4), (6, 0), (0, 4))
OFF, DIAG = len(LEVELS), len(LEVELS) + 1
NLEV = len(LEVELS) + 2
GAIN_ROWS = 5 * KC + NPAIR

(G_F, G_Q, M_Q, M_K, M_V, G_I, G_G, X_K0, X_K1, X_V0,
 W_O0, W_O1, X_V1, X_Q0, X_Q1, C_O0, C_O1) = range(17)
FEATURE_GROUPS = (G_F, G_Q, M_Q, M_K, X_K0, X_K1, X_Q0, X_Q1)


def mixing_schedule():
    small = []
    for l in range(NLEV):
        small.append(("decay", l))
        small.append(("level", l))
    heads = []
    for i in range(NH + 2):
        if i < NH:
            heads.append(("score", i))
        if i >= 2:
            heads.append(("out", i - 2))
        if 1 <= i <= NH:
            heads.append(("turn", i - 1))
    filler = [("proj", g, j) for g in (M_V, G_I, G_G, X_K0, X_K1, X_V0) for j in range(4)]
    order, level_at, head_at = [], 0, 0
    for n, f in enumerate(filler):
        order.append(f)
        while level_at < len(small) and level_at * 22 <= n * len(small):
            order.append(small[level_at])
            level_at += 1
        while n >= 4 and head_at < len(heads) and head_at * 19 <= (n - 4) * len(heads):
            order.append(heads[head_at])
            head_at += 1
    return order + small[level_at:] + heads[head_at:]


def build(nc, x, mem, ln_mix_g, w_in, hgrn_lb_logits, hgrn_norm_g, w_out, ln_x_g, ln_mem_g, wq_x,
          wkv_x, wo_x, ln_moe_g, w_router, b_router, w1, b1, w2, b2, ln_f_g, out):
    ctx = ExitStack()
    with ctx:
        def sb(name, shape, dt=F32):
            return ctx.enter_context(nc.sbuf_tensor(name, shape, dt))

        def sem(name):
            return ctx.enter_context(nc.semaphore(name))

        expert_ring = sb("expert_ring", [P, EXPERT_UNITS, UNIT])
        front_ring = sb("front_ring", [P, 2 * FRONT_PAIRS, UNIT])
        h = sb("h", [P, TT, D])
        hn = sb("hn", [P, TT, D])
        hnT = sb("hnT", [P, KC, T])
        KxT = sb("KxT", [P, KC, T])
        Vx = sb("Vx", [P, TT, D])
        qxT = sb("qxT", [P, KC, T])
        pbuf = sb("pbuf", [P, 1536])

        hits = pbuf[:, 0:TT * NE * TOPK].rearrange("p (t e j) -> p t e j", t=TT, e=NE)
        logitsT = pbuf[:, 256:512]
        zeros_b = pbuf[:, 1280:1536].bitcast(BF16)

        def scratch(slot, a=0, b=UNIT):
            return expert_ring[:, slot, a:b]
        mem_sb = scratch(0).rearrange("p (t d) -> p t d", t=TT)
        mixT = scratch(0).rearrange("p (c t) -> p c t", c=KC)
        memT = scratch(1).rearrange("p (c t) -> p c t", c=KC)
        mqT = scratch(2, 0, 1024).rearrange("p (c t) -> p c t", c=NPAIR)
        mkT = scratch(2, 1024).rearrange("p (c t) -> p c t", c=NPAIR)
        mv = scratch(3, 0, 1024).rearrange("p (t d) -> p t d", t=TT)
        gi = scratch(3, 1024).rearrange("p (t d) -> p t d", t=TT)
        sgate = scratch(4, 0, 1024)
        bsum = scratch(4, 1024)
        gq = scratch(5, 0, 1024)
        fgate = scratch(5, 1024)
        kgate = scratch(6, 0, 1024)
        tmp = scratch(6, 1024)
        factor = [scratch(7, 0, 1024), scratch(7, 1024)]
        factor_pad = scratch(8).rearrange("p (c j t) -> p c j t", c=NPAIR, j=2)
        mem_n = scratch(8).rearrange("p (t d) -> p t d", t=TT)
        squares = scratch(8)
        a_in = scratch(9)
        a_off = scratch(10, 0, 1024)
        lmask = scratch(10, 1024).bitcast(I32).rearrange("p (l t) -> p l t", l=8)
        mix = scratch(11).rearrange("p (t d) -> p t d", t=TT)

        ident = sb("ident", [P, P])
        before = sb("before", [P, P])
        cmask = sb("cmask", [P, 3, P])
        iota_i = factor[1][:, 0:2 * P].rearrange("p (n t) -> p n t", n=2).bitcast(I32)
        xor_f = factor[1][:, 2 * P:3 * P]
        iota_s = sb("iota_s", [P, T])
        eps = sb("eps", [P, 1])
        gain_cols = sb("gain_cols", [P, GAIN_ROWS])
        gains = gain_cols[:, 0:4 * KC].rearrange("p (n c) -> p n c", n=4)
        lbl = gain_cols[:, 4 * KC:5 * KC].rearrange("p (r c) -> p r c", r=2)
        hg_gain = gain_cols[:, 5 * KC:GAIN_ROWS]
        gain_rows = pbuf[0:GAIN_ROWS, 0:P]
        lb = sb("lb", [P, 6, NPAIR])
        ssq = sb("ssq", [P, TT, 2])
        half_ms = sb("half_ms", [P, TT])
        std = sb("std", [P, TT])
        rstd = sb("rstd", [P, TT])
        hg_ssq = sb("hg_ssq", [P, 2 * NH])
        hg_rstd = sb("hg_rstd", [P, 2 * NH])
        mx = sb("mx", [P, 2, TT])
        nmx = sb("nmx", [P, 2, TT])
        psum_row = sb("psum_row", [P, 2, TT])
        rinv = sb("rinv", [P, 2, TT])
        wr = sb("wr", [P, KC, 64])
        br = sb("br", [P, NE])
        fold = sb("fold", [P, NE])
        logits = sb("logits", [P, TT, NE])
        elog = sb("elog", [P, TT, NE])
        top8 = sb("top8", [P, TT, 8])
        idx8 = sb("idx8", [P, TT, 8], U32)
        idx8f = sb("idx8f", [P, TT, 8])
        sel = sb("sel", [P, TT, NE], BF16)
        before_b = sb("before_b", [P, P], BF16)
        ones_b = sb("ones_b", [P, P], BF16)
        ntop = sb("ntop", [P, TT])
        gate_sum = sb("gate_sum", [P, TT])
        posm = sb("posm", [P, TT, NE + 1])
        tabf = sb("tabf", [1, 5, NE])
        tab = sb("tab", [1, 2, NE], I32)

        ring_row = front_ring[:, :, :].rearrange("p u n -> p (u n)")
        at = [0]

        def loop_buf(n):
            at[0] += n
            assert at[0] <= 2 * FRONT_PAIRS * UNIT
            return ring_row[:, at[0] - n:at[0]]
        xn_part = [loop_buf(D).bitcast(BF16).rearrange("p (t d) -> p t d", t=TT) for _ in range(3)]
        xgT = loop_buf(KC * SLOTS).rearrange("p (c s) -> p c s", c=KC)
        xgT_more = loop_buf(KC * SLOTS).rearrange("p (c s) -> p c s", c=KC)
        glu, lin, sig, actb, y_sb = (loop_buf(GW) for _ in range(5))
        actT = loop_buf(GW).rearrange("p (q j s) -> p q j s", q=4, j=2)
        pick_gated = loop_buf(TT * P).rearrange("p (t n s) -> p t n s", t=TT, n=2)
        pick = loop_buf(TT * SLOTS // 2).bitcast(BF16).rearrange("p (t s) -> p t s", t=TT)
        b1_pick, b2_pick = loop_buf(SLOTS), loop_buf(SLOTS)
        gates = loop_buf(TT * NE).rearrange("p (t e) -> p t e", t=TT)
        lnf = loop_buf(D)
        assert at[0] >= 2 * (X_Q1 % FRONT_PAIRS) * UNIT and X_Q1 % FRONT_PAIRS == FRONT_PAIRS - 1
        b1_sb = loop_buf(2 * D)
        b2_sb = loop_buf(D)
        sgT = loop_buf(2 * T).rearrange("p (n t) -> p n t", n=2)
        odd_slot = [KxT[:, :, :].rearrange("p c t -> p (c t)"), Vx[:, :, :].rearrange("p t d -> p (t d)"),
                    qxT[:, :, :].rearrange("p c t -> p (c t)"), hnT[:, :, :].rearrange("p c t -> p (c t)")]

        ps = ctx.enter_context(nc.psum_tensor("ps", [P, 8, 512], F32))

        def banks(a, b):
            return ps[:, a:b, :]

        x_loaded = [sem(f"x_loaded{t}") for t in range(TT)]
        mem_loaded = sem("mem_loaded")
        small_loaded = sem("small_loaded")
        router_loaded = sem("router_loaded")
        unit_loaded = [sem(f"unit_loaded{s}") for s in range(2 * FRONT_PAIRS)]
        expert_loaded = [sem(f"expert_loaded{s}") for s in range(EXPERT_UNITS)]
        odd_loaded = [sem(f"odd_loaded{v}") for v in range(4)]
        gains_turned = sem("gains_turned")
        rows_done, rows_final = sem("rows_done"), sem("rows_final")
        logits_done, logitsT_ready = sem("logits_done"), sem("logitsT_ready")
        bias_loaded, lnf_loaded, out_stored = sem("bias_loaded"), sem("lnf_loaded"), sem("out_stored")
        pool_chain, act_chain, dve_chain = sem("pool_chain"), sem("act_chain"), sem("dve_chain")
        consts_ready, masks_ready = sem("consts_ready"), sem("masks_ready")
        pads_zeroed, loop_zeroed = sem("pads_zeroed"), sem("loop_zeroed")
        rows_squared, std_ready, hn_ready = sem("rows_squared"), sem("std_ready"), sem("hn_ready")
        hn_turned, hnT_ready = sem("hn_turned"), sem("hnT_ready")
        group_done, group_kept = sem("group_done"), sem("group_kept")
        forget_kept, gate_ready, log_ready = sem("forget_kept"), sem("gate_ready"), sem("log_ready")
        lb_exp = sem("lb_exp")
        diff_ready, decay_ready = sem("diff_ready"), sem("decay_ready")
        factor_ready, pad_ready = sem("factor_ready"), sem("pad_ready")
        level_done, level_kept = sem("level_done"), sem("level_kept")
        score_done, score_kept, prob_ready = sem("score_done"), sem("score_kept"), sem("prob_ready")
        prob_turned, probT_ready = sem("prob_turned"), sem("probT_ready")
        head_done, head_kept, rinv_ready = sem("head_done"), sem("head_kept"), sem("rinv_ready")
        hg_done, hg_squared, hg_summed = sem("hg_done"), sem("hg_squared"), sem("hg_summed")
        hg_std, hg_mix_ready = sem("hg_std"), sem("hg_mix_ready")
        mix_turned, mixT_ready = sem("mix_turned"), sem("mixT_ready")
        residual_ready = sem("residual_ready")
        xs_done, xs_max, xs_prob, xs_scaled = sem("xs_done"), sem("xs_max"), sem("xs_prob"), sem("xs_scaled")
        xp_turned, xpT_ready = sem("xp_turned"), sem("xpT_ready")
        xo_done, xo_kept = sem("xo_done"), sem("xo_kept")
        router_done, router_max, router_exp, chosen = (
            sem("router_done"), sem("router_max"), sem("router_exp"), sem("chosen"))
        ranked, top_found = sem("ranked"), sem("top_found")
        table_ready = sem("table_ready")
        part_ready = [sem(f"part_ready{t}") for t in range(TT)]
        rest_ready = [sem(f"rest_ready{t}") for t in range(TT)]
        tile0_scattered = sem("tile0_scattered")
        pick_ready, pickg_ready, b1_pick_ready = sem("pick_ready"), sem("pickg_ready"), sem("b1_pick_ready")
        bias_added, gathered, xgT_ready = sem("bias_added"), sem("gathered"), sem("xgT_ready")
        b2_pick_ready = sem("b2_pick_ready")
        up_used, glu_ready, sig_ready, act_ready = sem("up_used"), sem("glu_ready"), sem("sig_ready"), sem("act_ready")
        act_turned, actT_ready = sem("act_turned"), sem("actT_ready")
        pickg_turned, sgT_ready = sem("pickg_turned"), sem("sgT_ready")
        down_used, y_ready, scattered = sem("down_used"), sem("y_ready"), sem("scattered")
        dve_loop, act_loop = sem("dve_loop"), sem("act_loop")
        m_pick, m_gathered, m_xgT, m_up, m_glu, m_sig, m_act = (
            sem(f"more_{n}") for n in ("pick", "gathered", "xgT", "up", "glu", "sig", "act"))
        m_turned, m_sgT, m_actturn, m_actT, m_down, m_y, m_scattered = (
            sem(f"more_{n}") for n in ("turned", "sgT", "actturn", "actT", "down", "y", "scattered"))
        m_lin, m_dve, m_closed = sem("more_lin"), sem("more_dve"), sem("more_closed")

        def linker(eng, s):
            n = [0]

            def link(ins):
                n[0] += 1
                ins.then_inc(s, 1)
                eng.wait_ge(s, n[0])
            return link

        order = mixing_schedule()
        level_order = list(range(NLEV))

        def group_weights(g):
            if g <= G_G:
                return w_in, {G_F: 4, G_Q: 3, M_Q: 0, M_K: 1, M_V: 2, G_I: 5, G_G: 6}[g] * GW
            if g in (X_K0, X_K1, X_V0, X_V1):
                return wkv_x, {X_K0: 0, X_K1: 1, X_V0: 2, X_V1: 3}[g] * GW
            if g <= W_O1:
                return w_out, (g - W_O0) * GW
            if g <= X_Q1:
                return wq_x, (g - X_Q0) * GW
            return wo_x, (g - C_O0) * GW

        def kept_count(g):
            return g + 1 - (2 if g > W_O1 else 0)

        def group_unit(g, k):
            slot = 2 * (g % FRONT_PAIRS) + k // 4
            return front_ring[:, slot, (k % 4) * GW:(k % 4 + 1) * GW]

        def group_arrived(eng, g, half):
            eng.wait_ge(unit_loaded[2 * (g % FRONT_PAIRS) + half], 16 * (g // FRONT_PAIRS + 1))

        def mp(i):
            return pbuf[:, (i % 2) * 384:(i % 2 + 1) * 384]

        def mpT(i):
            return pbuf[:, 768 + (i % 2) * 384:768 + (i % 2 + 1) * 384]

        def xp(i):
            return pbuf[:, (i % 2) * 512:(i % 2 + 1) * 512].rearrange("p (t k) -> p t k", t=TT)
        xpT = pbuf[:, 1024:1536].rearrange("p (k q) -> p k q", k=TT)

        def blocks_of(ap, m):
            v = ap.rearrange("p (n two m) -> p n two m", two=2, m=m)
            return v[:, :, 0, :], v[:, :, 1, :]

        block = ctx.enter_context(nc.Block())

        @block.sync
        def _(sp):
            for t in range(TT):
                sp.dma_start(h[:, t, :], x[0, t * P:(t + 1) * P, :]).then_inc(x_loaded[t], 16)
            gain_sources = [(n * KC, KC, g[0].rearrange("(c p) -> c p", p=P))
                            for n, g in enumerate((ln_mix_g, ln_mem_g, ln_x_g, ln_moe_g))]
            gain_sources += [(4 * KC, KC, hgrn_lb_logits.rearrange("r (c p) -> (r c) p", p=P)),
                             (5 * KC, NPAIR, hgrn_norm_g[0].rearrange("(c p) -> c p", p=P))]
            for row, n, src in gain_sources:
                sp.dma_start(gain_rows[row:row + n, :], src).then_inc(small_loaded, 16)
            for g in range(C_O1 + 1):
                if g == G_Q:
                    sp.dma_start(mem_sb, mem[0].rearrange("(t p) d -> p t d", p=P)).then_inc(mem_loaded, 16)
                elif g == M_Q:
                    sp.wait_ge(masks_ready, 9)
                    sp.dma_start(wr[:, :, 0:NE], w_router[0].rearrange("(c p) e -> p c e", p=P)).then_inc(router_loaded, 16)
                    sp.dma_start(br[:, :], b_router[0].partition_broadcast(P)).then_inc(router_loaded, 16)
                src, col = group_weights(g)
                if g >= FRONT_PAIRS:
                    sp.wait_ge(group_done, g - FRONT_PAIRS + 1)
                for half in range(2):
                    sp.dma_start(
                        front_ring[:, 2 * (g % FRONT_PAIRS) + half, :].rearrange("p (k n) -> p k n", k=4),
                        src[0, half * 512:(half + 1) * 512, col:col + GW].rearrange("(k p) n -> p k n", p=P),
                    ).then_inc(unit_loaded[2 * (g % FRONT_PAIRS) + half], 16)

            def load_up(e, u):
                sp.dma_start(expert_ring[:, u, :], w1[0, e, u * P:(u + 1) * P, :]).then_inc(expert_loaded[u], 16)

            def load_down(e, odd, v):
                dst = odd_slot[v] if odd else expert_ring[:, 8 + v, :]
                sp.dma_start(dst.rearrange("p (a n) -> p a n", a=2),
                             w2[0, e, v * 2 * P:(v + 1) * 2 * P, :].rearrange("(a p) n -> p a n", p=P)
                             ).then_inc(odd_loaded[v] if odd else expert_loaded[8 + v], 16)

            sp.wait_ge(residual_ready, 4)
            for u in range(8):
                load_up(0, u)
            for v in range(4):
                load_down(0, 0, v)
            for v in range(4):
                if v == 0:
                    sp.wait_ge(xs_done, XH)
                elif v == 1:
                    sp.wait_ge(xo_done, XH)
                elif v == 2:
                    sp.wait_ge(group_done, C_O1 + 1)
                else:
                    sp.wait_ge(router_done, 1)
                load_down(1, 1, v)
            for u in range(8):
                sp.wait_ge(up_used, u + 1)
                load_up(1, u)
            with sp.Fori(0, NE // 2 - 1) as pair:
                for odd in range(2):
                    e = pair * 2 + (2 + odd)
                    for u in range(8):
                        sp.wait_ge(up_used, pair * 16 + (8 * (1 + odd) + u + 1))
                        load_up(e, u)
                    for v in range(4):
                        sp.wait_ge(down_used, pair * 8 + (4 * odd + v + 1))
                        load_down(e, odd, v)

            for t in range(TT):
                sp.wait_ge(rows_final, t + 1)
                sp.dma_start(out[0, t * P:(t + 1) * P, :], hn[:, t, :]).then_inc(out_stored, 16)
            sp.wait_ge(out_stored, 16 * TT)

        @block.gpsimd
        def _(pool):
            def step(ins, done, n):
                ins.then_inc(done, 1)
                pool.wait_ge(done, n)

            step(nc.gpsimd.memset(ident[:, :], 0.0), pool_chain, 1)
            step(nc.gpsimd.affine_select(out=ident[:, :], in_=ident[:, :], compare_op=ALU.not_equal, fill=1.0,
                                         base=0, pattern=[[-1, P]], channel_multiplier=1), consts_ready, 1)
            step(nc.gpsimd.memset(eps[:, :], EPS), consts_ready, 2)
            step(nc.gpsimd.memset(before[:, :], 1.0), pool_chain, 2)
            step(nc.gpsimd.affine_select(out=before[:, :], in_=before[:, :], compare_op=ALU.is_gt, fill=0.0,
                                         base=0, pattern=[[1, P]], channel_multiplier=-1), masks_ready, 1)
            step(nc.gpsimd.memset(cmask[:, :, :], 0.0), pool_chain, 3)
            for n, c in enumerate((0, 2)):
                step(nc.gpsimd.affine_select(out=cmask[:, c, :], in_=cmask[:, c, :], compare_op=ALU.is_ge,
                                             fill=MASKED, base=0, pattern=[[-1, P]],
                                             channel_multiplier=1), masks_ready, 2 + n)
            step(nc.gpsimd.iota(iota_i[:, 0, :], pattern=[[1, P]], base=0, channel_multiplier=0), masks_ready, 4)
            step(nc.gpsimd.iota(iota_i[:, 1, :], pattern=[[0, P]], base=0, channel_multiplier=1), masks_ready, 5)
            step(nc.gpsimd.iota(iota_s[:, :], pattern=[[1, T]], base=0, channel_multiplier=0,
                                allow_small_or_imprecise_dtypes=True), masks_ready, 6)
            step(nc.gpsimd.memset(posm[:, :, NE:NE + 1], -1.0), masks_ready, 7)
            step(nc.gpsimd.memset(ones_b[:, :], 1.0), masks_ready, 8)
            step(nc.gpsimd.memset(wr[:, :, NE:64], 0.0), masks_ready, 9)
            pool.wait_ge(hn_turned, 8)
            for j in range(2):
                step(nc.gpsimd.memset(factor_pad[64 * j:64 * j + 64, :, 1 - j, :], 0.0), pads_zeroed, j + 1)
            pool.wait_ge(group_done, X_Q1 + 1)
            zeroed = [b[p:p + n, :] for b in (b1_sb, b2_sb) for p, n in ((32, 32), (64, 64))]
            zeroed += [sgT[64 * n:64 * n + 64, 1 - n, :] for n in range(2)]
            for n, rows in enumerate(zeroed):
                step(nc.gpsimd.memset(rows, 0.0), loop_zeroed, n + 1)
            pool.dma_start(b1_sb[0:NE, :], b1[0]).then_inc(bias_loaded, 16)
            pool.dma_start(b2_sb[0:NE, :], b2[0]).then_inc(bias_loaded, 16)
            pool.wait_ge(group_done, C_O1 + 1)
            step(nc.gpsimd.memset(zeros_b, 0.0), loop_zeroed, 7)
            pool.wait_ge(part_ready[0], 1)
            pool.wait_ge(hn_turned, 14)
            step(nc.gpsimd.tensor_tensor(hn[:, 0, :], hn[:, 0, :], xn_part[0][:, 0, :], ALU.subtract), rest_ready[0], 1)
            for t in range(TT):
                pool.wait_ge(part_ready[t], 2)
                step(nc.gpsimd.tensor_tensor(xn_part[2][:, t, :], hn[:, t, :], xn_part[1][:, t, :], ALU.subtract),
                     rest_ready[t], 2)
            pool.dma_start(lnf, ln_f_g.partition_broadcast(P)).then_inc(lnf_loaded, 16)
            pool.wait_ge(bias_loaded, 32)
            pool.wait_ge(lnf_loaded, 16)

        @block.scalar
        def _(act):
            def norm_stats(n, src, scratch_of, arrived):
                if n >= 1:
                    act.wait_ge(hn_ready, 2 * n)
                for t in range(TT):
                    for half in range(2):
                        arrived(t, half)
                        nc.scalar.activation(scratch_of(t, half), src[:, t, half * GW:(half + 1) * GW], ACT.Square,
                                             accum_out=ssq[:, t, half:half + 1]).then_inc(rows_squared, 1)
                        if half == 0:
                            act.wait_ge(rows_squared, 6 * n + 3 * t + 1)
                            nc.scalar.activation(half_ms[:, t:t + 1], ssq[:, t, 0:1], ACT.Identity, bias=eps[:, :],
                                                 scale=1.0 / D).then_inc(rows_squared, 1)
                    act.wait_ge(rows_squared, 6 * n + 3 * t + 3)
                    nc.scalar.activation(std[:, t:t + 1], ssq[:, t, 1:2], ACT.Sqrt, bias=half_ms[:, t:t + 1],
                                         scale=1.0 / D).then_inc(std_ready, 1)

            def in_rows(buf):
                return lambda t, half: buf[:, t, half * GW:(half + 1) * GW]

            def residual_added(n):
                return lambda t, half: act.wait_ge(residual_ready, 4 * n + 2 * t + half + 1)

            act.wait_ge(consts_ready, 2)
            nc.scalar.activation(half_ms[:, 0:1], eps[:, :], ACT.Sqrt).then_inc(act_chain, 1)
            act.wait_ge(act_chain, 1)
            norm_stats(0, h, in_rows(hn), lambda t, half: act.wait_ge(x_loaded[t], 16))
            norm_stats(1, mem_sb, in_rows(mem_n), lambda t, half: act.wait_ge(mem_loaded, 16))
            act.wait_ge(lb_exp, 1)
            nc.scalar.activation(lb[:, 2:4, :], lb[:, 0:2, :], ACT.Exp).then_inc(lb_exp, 1)

            def keep_group(g, a, dst):
                act.wait_ge(group_done, g + 1)
                return nc.scalar.activation(dst, banks(a, a + 2).rearrange("p b n -> p (b n)"), ACT.Copy)

            act.wait_ge(group_done, G_F + 1)
            nc.scalar.activation(fgate, banks(0, 2).rearrange("p b n -> p (b n)"), ACT.Exp,
                                 scale=-1.0).then_inc(group_kept, 1)
            keep_group(G_Q, 2, gq).then_inc(group_kept, 1)
            act.wait_ge(group_kept, 2)
            nc.scalar.activation(tmp, gq, ACT.Exp, scale=-1.0).then_inc(gate_ready, 1)
            keep_group(M_Q, 0, mqT.rearrange("p c t -> p (c t)")).then_inc(group_kept, 1)
            act.wait_ge(log_ready, 1)
            nc.scalar.activation(tmp, fgate, ACT.Ln).then_inc(log_ready, 1)
            keep_group(M_K, 2, mkT.rearrange("p c t -> p (c t)")).then_inc(group_kept, 1)

            def decay_exp(l):
                act.wait_ge(diff_ready, l + 1)
                nc.scalar.activation(factor[l % 2], factor[l % 2], ACT.Exp).then_inc(decay_ready, 1)
            act.wait_ge(pads_zeroed, 2)
            decay_exp(0)
            for item in order:
                kind, i = item[0], item[1]
                if kind == "proj" and item[2] == 3:
                    if i in (M_V, G_I):
                        dst = {M_V: mv, G_I: gi}[i].rearrange("p t d -> p (t d)")
                        keep_group(i, 0, dst).then_inc(group_kept, 1)
                    elif i == G_G:
                        keep_group(i, 0, sgate).then_inc(group_kept, 1)
                        act.wait_ge(group_kept, G_G + 1)
                        nc.scalar.activation(tmp, sgate, ACT.Exp, scale=-1.0).then_inc(gate_ready, 1)
                    elif i in (X_K0, X_K1):
                        dst = KxT[:, 4 * (i - X_K0):4 * (i - X_K0) + 4, :].rearrange("p c t -> p (c t)")
                        keep_group(i, 0, dst).then_inc(group_kept, 1)
                    else:
                        act.wait_ge(group_done, X_V0 + 1)
                        nc.scalar.activation(Vx[:, :, 0:GW], banks(0, 2), ACT.Copy).then_inc(group_kept, 1)
                elif kind == "decay":
                    if i + 1 <= OFF:
                        decay_exp(i + 1)
                    if i != DIAG:
                        act.wait_ge(factor_ready, i + 1)
                        src = factor[i % 2]
                    else:
                        src = gq
                    if i >= 1:
                        act.wait_ge(level_done, 2 * i)
                    for j in range(2):
                        nc.scalar.activation(
                            factor_pad[64 * j:64 * j + 64, :, j, :],
                            src[64 * j:64 * j + 64, :].rearrange("p (c t) -> p c t", c=NPAIR),
                            ACT.Copy).then_inc(pad_ready, 1)
                elif kind == "score":
                    act.wait_ge(score_kept, i + 1)
                    if i >= 2:
                        act.wait_ge(rinv_ready, i - 1)
                    for t in range(TT):
                        row = mp(i)[:, 0:128] if t == 0 else mp(i)[:, 128:384]
                        nc.scalar.activation(row, row, ACT.Exp, bias=nmx[:, i % 2, t:t + 1],
                                             accum_out=psum_row[:, i % 2, t:t + 1]).then_inc(prob_ready, 1)
                elif kind == "turn":
                    act.wait_ge(prob_turned, i + 1)
                    if i >= 2:
                        act.wait_ge(head_done, i - 1)
                    nc.scalar.activation(mpT(i), ps[:, 7, 0:384], ACT.Copy).then_inc(probT_ready, 1)

            act.wait_ge(hg_done, 1)
            act.wait_ge(level_done, 2 * NLEV)
            nc.scalar.activation(squares[:, 0:1024], banks(4, 6).rearrange("p b n -> p (b n)"),
                                 ACT.Square).then_inc(hg_squared, 1)
            act.wait_ge(hg_summed, 1)
            nc.scalar.activation(hg_rstd[:, :], hg_ssq[:, :], ACT.Sqrt, bias=eps[:, :],
                                 scale=1.0 / HD).then_inc(hg_std, 1)

            norm_stats(2, h, in_rows(hn), residual_added(0))
            act.wait_ge(group_done, X_V1 + 1)
            nc.scalar.activation(Vx[:, :, GW:2 * GW], banks(4, 6), ACT.Copy).then_inc(group_kept, 1)
            keep_group(X_Q0, 2, qxT[:, 0:4, :].rearrange("p c t -> p (c t)")).then_inc(group_kept, 1)

            def exp_scores(i):
                act.wait_ge(xs_max, i + 1)
                if i >= 2:
                    act.wait_ge(xp_turned, i - 1)
                for t in range(TT):
                    nc.scalar.activation(xp(i)[:, t, :], ps[:, i % 2, t * T:(t + 1) * T], ACT.Exp,
                                         bias=nmx[:, i % 2, t:t + 1], scale=XHD ** -0.5,
                                         accum_out=psum_row[:, i % 2, t:t + 1]).then_inc(xs_prob, 1)

            def keep_probs(n):
                act.wait_ge(xp_turned, n + 1)
                if n >= 1:
                    act.wait_ge(xo_done, n)
                nc.scalar.activation(xpT.rearrange("p k q -> p (k q)"), ps[:, 4, :], ACT.Copy).then_inc(xpT_ready, 1)

            exp_scores(0)
            exp_scores(1)
            keep_probs(0)
            keep_group(X_Q1, 6, qxT[:, 4:8, :].rearrange("p c t -> p (c t)")).then_inc(group_kept, 1)
            keep_probs(1)
            exp_scores(2)
            exp_scores(3)
            keep_probs(2)
            keep_probs(3)
            norm_stats(3, h, in_rows(hn), residual_added(1))
            act.wait_ge(group_done, C_O1 + 1)
            for t in range(TT):
                act.wait_ge(hn_ready, 7 + t)
                nc.scalar.activation(xn_part[0][:, t, :], hn[:, t, :], ACT.Copy).then_inc(part_ready[t], 1)
            for t in range(TT):
                act.wait_ge(rest_ready[t], 1)
                nc.scalar.activation(xn_part[1][:, t, :], hn[:, t, :], ACT.Copy).then_inc(part_ready[t], 1)
            act.wait_ge(router_max, 1)
            for t in range(TT):
                nc.scalar.activation(elog[:, t, :], logits[:, t, :], ACT.Exp,
                                     bias=ntop[:, t:t + 1]).then_inc(router_exp, 1)

            def keep_sgT(done):
                for n in range(2):
                    last = nc.scalar.activation(sgT[64 * n:64 * n + 64, n, :], ps[64 * n:64 * n + 64, 7, 0:T],
                                                ACT.Copy)
                last.then_inc(done, 1)

            act.wait_ge(loop_zeroed, 7)
            act.wait_ge(table_ready, 1)
            act.sem_inc(actT_ready, 1)
            with act.Fori(0, NE) as e:
                count = act.value_load(tab[0:1, 0, bass.ds(e, 1)], min_val=0, max_val=T)
                with act.If(count > SLOTS):
                    first = act.value_load(tab[0:1, 1, bass.ds(e, 1)], min_val=0, max_val=NE)
                    with act.Fori(1, MAXBLK) as q:
                        with act.If(count > q * SLOTS):
                            n = first + q
                            act.wait_ge(m_turned, n)
                            act.wait_ge(scattered, e + 1)
                            keep_sgT(m_sgT)
                            act.wait_ge(m_glu, n)
                            nc.scalar.activation(sig, glu, ACT.Sigmoid, scale=ALPHA).then_inc(m_sig, 1)
                            act.wait_ge(m_actturn, n)
                            nc.scalar.activation(actT.rearrange("p q j s -> p (q j s)"), ps[:, 7, :],
                                                 ACT.Copy).then_inc(m_actT, 1)
                            act.wait_ge(m_scattered, n)
                            act.sem_inc(m_closed, 1)
                act.wait_ge(glu_ready, e + 1)
                nc.scalar.activation(sig, glu, ACT.Sigmoid, scale=ALPHA).then_inc(sig_ready, 1)
                act.wait_ge(pickg_turned, e + 2)
                act.wait_ge(scattered, e + 1)
                keep_sgT(sgT_ready)
                act.wait_ge(act_turned, e + 2)
                nc.scalar.activation(actT.rearrange("p q j s -> p (q j s)"), ps[:, 7, :],
                                     ACT.Copy).then_inc(actT_ready, 1)
            norm_stats(4, h, lambda t, half: (glu, lin, sig, actb)[2 * t + half], residual_added(2))

        @block.vector
        def _(dve):
            link = linker(dve, dve_chain)

            def norm_rows(n, t, src, dst):
                dve.wait_ge(std_ready, 2 * n + t + 1)
                link(nc.vector.reciprocal(rstd[:, t:t + 1], std[:, t:t + 1]))
                nc.vector.tensor_scalar(dst[:, t, :], src[:, t, :], rstd[:, t:t + 1], None,
                                        ALU.mult).then_inc(hn_ready, 1)

            def norm_gain(n, t, dst):
                for half in range(2):
                    dve.wait_ge(hn_turned, 4 * n + 2 * t + half + 1)
                    g = gains[:, n, 4 * half:4 * half + 4].unsqueeze(2).to_broadcast([P, 4, P])
                    src = ps[:, TURN_BANKS[n][t] + half, :].rearrange("p (c q) -> p c q", c=4)
                    nc.vector.tensor_tensor(dst[:, 4 * half:4 * half + 4, t * P:(t + 1) * P], src, g,
                                            ALU.mult).then_inc(hnT_ready, 1)

            dve.wait_ge(gains_turned, 1)
            nc.vector.tensor_copy(gain_cols[:, :], ps[:, 0, 0:GAIN_ROWS]).then_inc(gains_turned, 1)
            for t in range(TT):
                norm_rows(0, t, h, hn)
            dve.wait_ge(gains_turned, 2)
            for t in range(TT):
                norm_gain(0, t, hnT)
            for t in range(TT):
                norm_rows(1, t, mem_sb, mem_n)
            link(nc.vector.tensor_tensor(lb[:, 4, :], lbl[:, 0, :], lbl[:, 1, :], ALU.max))
            for r in range(2):
                ins = nc.vector.tensor_tensor(lb[:, r, :], lbl[:, r, :], lb[:, 4, :], ALU.subtract)
                if r == 0:
                    link(ins)
            ins.then_inc(lb_exp, 1)
            dve.wait_ge(masks_ready, 9)
            link(nc.vector.tensor_tensor(iota_i[:, 0, :], iota_i[:, 0, :], iota_i[:, 1, :], ALU.bitwise_xor))
            link(nc.vector.tensor_copy(xor_f, iota_i[:, 0, :]))
            link(nc.vector.tensor_tensor(xor_f, xor_f, before[:, :], ALU.mult))
            for l, m in enumerate(LEVELS):
                link(nc.vector.tensor_scalar(factor[0][:, 0:P], xor_f, float(m), None, ALU.is_ge))
                link(nc.vector.scalar_tensor_tensor(out=lmask[:, l, :], in0=xor_f, scalar=float(2 * m),
                                                    in1=factor[0][:, 0:P], op0=ALU.is_lt, op1=ALU.mult))
            link(nc.vector.tensor_copy(lmask[:, 7, :], ident[:, :]))
            link(nc.vector.memset(a_in, 0.0))
            link(nc.vector.tensor_copy(before_b[:, :], before[:, :]))
            link(nc.vector.tensor_tensor(fold[:, :], ident[:, 0:NE], ident[:, 64:64 + NE], ALU.add))
            for t in range(TT):
                norm_gain(1, t, memT)
            dve.wait_ge(lb_exp, 2)
            link(nc.vector.tensor_tensor(lb[:, 4, :], lb[:, 2, :], lb[:, 3, :], ALU.add))
            link(nc.vector.reciprocal(lb[:, 5, :], lb[:, 4, :]))
            link(nc.vector.tensor_tensor(lb[:, 0, :], lb[:, 2, :], lb[:, 5, :], ALU.mult))
            link(nc.vector.tensor_scalar(lb[:, 1, :], lb[:, 0, :], -1.0, 1.0, ALU.mult, ALU.add))
            dve.wait_ge(group_kept, G_F + 1)
            link(nc.vector.tensor_scalar_add(fgate, fgate, 1.0))
            link(nc.vector.reciprocal(fgate, fgate))
            for c in range(NPAIR):
                cols = slice(c * T, (c + 1) * T)
                link(nc.vector.tensor_scalar(fgate[:, cols], fgate[:, cols], lb[:, 1, c:c + 1],
                                             lb[:, 0, c:c + 1], ALU.mult, ALU.add))
            dve.wait_ge(gate_ready, 1)
            link(nc.vector.tensor_scalar_add(tmp, tmp, 1.0))
            link(nc.vector.reciprocal(tmp, tmp))
            link(nc.vector.tensor_tensor(gq, gq, tmp, ALU.mult))
            nc.vector.tensor_scalar(kgate, fgate, -1.0, 1.0, ALU.mult, ALU.add).then_inc(log_ready, 1)
            link(nc.vector.memset(factor[1], 1.0))
            link(nc.vector.memset(factor[1].rearrange("p (n m) -> p n m", m=P)[:, :, 0:1], 0.0))
            dve.wait_ge(log_ready, 2)
            link(nc.vector.tensor_tensor_scan(bsum, factor[1], tmp, 0.0, ALU.mult, ALU.add))

            def differences(l):
                m = P if l == OFF else LEVELS[l]
                b1st, b2nd = blocks_of(bsum, m)
                f1st, f2nd = blocks_of(factor[l % 2], m)
                if l >= 2:
                    dve.wait_ge(pad_ready, 2 * (l - 1))
                    dve.wait_ge(level_done, 2 * (l - 1))
                mid = b1st[:, :, m - 1:m].to_broadcast([P, 1024 // (2 * m), m])
                if l == OFF:
                    link(nc.vector.tensor_copy(f2nd, b2nd))
                else:
                    link(nc.vector.tensor_tensor(f2nd, b2nd, mid, ALU.subtract))
                nc.vector.tensor_tensor(f1st, mid, b1st, ALU.subtract).then_inc(diff_ready, 1)

            differences(0)
            for item in order:
                kind, i = item[0], item[1]
                if kind == "proj" and i in (X_K0, X_K1):
                    dve.wait_ge(gate_ready, 2)
                    at8 = 4 * (i - X_K0) + item[2]
                    cols = slice(at8 * P, (at8 + 1) * P)
                    link(nc.vector.tensor_scalar_add(tmp[:, cols], tmp[:, cols], 1.0))
                    link(nc.vector.reciprocal(tmp[:, cols], tmp[:, cols]))
                    link(nc.vector.tensor_tensor(sgate[:, cols], sgate[:, cols], tmp[:, cols], ALU.mult))
                elif kind == "decay":
                    if i + 1 <= OFF:
                        differences(i + 1)
                    if i <= OFF:
                        dve.wait_ge(decay_ready, i + 1)
                        m = P if i == OFF else LEVELS[i]
                        f1st, f2nd = blocks_of(factor[i % 2], m)
                        link(nc.vector.tensor_tensor(f2nd, f2nd, blocks_of(gq, m)[1], ALU.mult))
                        nc.vector.tensor_tensor(f1st, f1st, blocks_of(kgate, m)[0], ALU.mult).then_inc(factor_ready, 1)
                elif kind == "level":
                    if i == OFF:
                        dve.wait_ge(level_done, 2 * i + 2)
                        nc.vector.tensor_copy(a_off, banks(2, 4).rearrange("p b n -> p (b n)")).then_inc(level_kept, 2)
                        continue
                    mask = lmask[:, 7 if i == DIAG else i, :].unsqueeze(1).to_broadcast([P, 2, P])
                    for half in range(2):
                        dve.wait_ge(level_done, 2 * i + half + 1)
                        for c in range(NPAIR):
                            ins = nc.vector.copy_predicated(
                                a_in.rearrange("p (c n j t) -> p c n j t", c=NPAIR, n=2, j=2)[:, c, half],
                                mask,
                                banks(2 + 2 * half, 4 + 2 * half).rearrange(
                                    "p b (c j t) -> p (b c) j t", c=2, j=2)[:, c])
                            if c < NPAIR - 1:
                                link(ins)
                        ins.then_inc(level_kept, 1)
                        dve.wait_ge(level_kept, 2 * i + half + 1)
                elif kind == "score":
                    dve.wait_ge(score_done, i + 1)
                    if i >= 2:
                        dve.wait_ge(prob_turned, i - 1)
                    for t in range(TT):
                        cols = slice(0, 128) if t == 0 else slice(128, 384)
                        link(nc.vector.tensor_tensor_reduce(
                            out=mp(i)[:, cols], in0=ps[:, 6, cols],
                            in1=cmask[:, :, :].rearrange("p a b -> p (a b)")[:, cols],
                            scale=HD ** -0.5, scalar=MASKED, op0=ALU.add, op1=ALU.max,
                            accum_out=mx[:, i % 2, t:t + 1]))
                    nc.vector.tensor_scalar(nmx[:, i % 2, :], mx[:, i % 2, :], -1.0, None,
                                            ALU.mult).then_inc(score_kept, 1)
                elif kind == "turn":
                    dve.wait_ge(prob_ready, 2 * i + 2)
                    if i >= 2:
                        dve.wait_ge(head_kept, i - 1)
                    nc.vector.reciprocal(rinv[:, i % 2, :], psum_row[:, i % 2, :]).then_inc(rinv_ready, 1)
                elif kind == "out":
                    dve.wait_ge(rinv_ready, i + 1)
                    dve.wait_ge(head_done, i + 1)
                    for t in range(TT):
                        ins = nc.vector.tensor_scalar(mix[:, t, i * HD:(i + 1) * HD],
                                                      ps[:, 7, 384 + t * HD:384 + (t + 1) * HD],
                                                      rinv[:, i % 2, t:t + 1], None, ALU.mult)
                        if t == 0:
                            link(ins)
                    ins.then_inc(head_kept, 1)

            dve.wait_ge(mix_turned, 1)
            nc.vector.tensor_copy(mixT[:, 0:4, :], banks(6, 8).rearrange("p b (c t) -> p (b c) t", c=2)).then_inc(mixT_ready, 1)
            dve.wait_ge(hg_squared, 1)
            nc.vector.tensor_reduce(hg_ssq[:, :], squares[:, 0:1024].rearrange("p (n d) -> p n d", d=HD),
                                    axis=AX_X, op=ALU.add).then_inc(hg_summed, 1)
            dve.wait_ge(hg_std, 1)
            link(nc.vector.reciprocal(hg_rstd[:, :], hg_rstd[:, :]))
            o_heads = banks(4, 6).rearrange("p b (n d) -> p (b n) d", d=HD)
            m_heads = squares[:, 1024:2048].rearrange("p (n d) -> p n d", d=HD)
            link(nc.vector.tensor_tensor(m_heads, o_heads,
                                         hg_rstd[:, :].unsqueeze(2).to_broadcast([P, 2 * NH, HD]), ALU.mult))
            nc.vector.tensor_tensor(mix[:, :, 512:1024], squares[:, 1024:2048].rearrange("p (t d) -> p t d", t=TT),
                                    sgate.rearrange("p (t d) -> p t d", t=TT), ALU.mult).then_inc(hg_mix_ready, 1)
            dve.wait_ge(mix_turned, 2)
            nc.vector.tensor_tensor(mixT[:, 4:8, :], banks(6, 8).rearrange("p b (c t) -> p (b c) t", c=2),
                                    hg_gain[:, :].unsqueeze(2).to_broadcast([P, NPAIR, T]),
                                    ALU.mult).then_inc(mixT_ready, 1)

            def add_residual(first_group, bank_of):
                earlier = 2 if first_group == C_O0 else 0
                norm = 2 if first_group == W_O0 else 3
                for t in range(TT):
                    for n in range(2):
                        if t == 0:
                            dve.wait_ge(rows_done, earlier + n + 1)
                        else:
                            dve.wait_ge(group_done, first_group + n + 1)
                        cols = slice(n * GW, (n + 1) * GW)
                        nc.vector.tensor_tensor(h[:, t, cols], ps[:, bank_of[n] + t, :], h[:, t, cols],
                                                ALU.add).then_inc(residual_ready, 1)
                        if t == 1 and n == 0:
                            norm_rows(norm, 0, h, hn)
                norm_rows(norm, 1, h, hn)
                for t in range(TT):
                    norm_gain(norm, t, hnT)

            add_residual(W_O0, (0, 2))
            def row_max(i):
                dve.wait_ge(xs_done, i + 1)
                if i >= 2:
                    dve.wait_ge(xs_prob, 2 * (i - 1))
                link(nc.vector.tensor_reduce(mx[:, i % 2, :], ps[:, i % 2, :].rearrange("p (t k) -> p t k", t=TT),
                                             axis=AX_X, op=ALU.max))
                nc.vector.tensor_scalar(nmx[:, i % 2, :], mx[:, i % 2, :], -XHD ** -0.5, None,
                                        ALU.mult).then_inc(xs_max, 1)

            def scale_probs(n):
                dve.wait_ge(xs_prob, 2 * n + 2)
                link(nc.vector.reciprocal(rinv[:, n % 2, :], psum_row[:, n % 2, :]))
                for t in range(TT):
                    nc.vector.tensor_scalar(xp(n)[:, t, :], xp(n)[:, t, :], rinv[:, n % 2, t:t + 1], None,
                                            ALU.mult).then_inc(xs_scaled, 1)

            def keep_output(n):
                dve.wait_ge(xo_done, n + 1)
                nc.vector.tensor_copy(qxT[:, 2 * n:2 * n + 2, :],
                                      ps[:, 5, :].rearrange("p (c q) -> p c q", c=2)).then_inc(xo_kept, 1)

            for first_head in (0, 2):
                for i in (first_head, first_head + 1):
                    row_max(i)
                    scale_probs(i)
                for i in (first_head, first_head + 1):
                    keep_output(i)
            add_residual(C_O0, (6, 2))

            dve.wait_ge(part_ready[1], 1)
            nc.vector.tensor_tensor(hn[:, 1, :], hn[:, 1, :], xn_part[0][:, 1, :], ALU.subtract).then_inc(rest_ready[1], 1)
            dve.wait_ge(router_done, 1)
            nc.vector.tensor_copy(logitsT, ps[:, 6, 0:T]).then_inc(logitsT_ready, 1)
            dve.wait_ge(logits_done, 1)
            dve.wait_ge(router_loaded, 32)
            link(nc.vector.tensor_tensor(logits[:, :, :], ps[:, 7, 0:TT * NE].rearrange("p (t e) -> p t e", t=TT),
                                         br[:, :].unsqueeze(1).to_broadcast([P, TT, NE]), ALU.add))
            for t in range(TT):
                ins = nc.vector.max(top8[:, t, :], logits[:, t, :])
                if t == 0:
                    ins.then_inc(top_found, 1)
            link(ins)
            dve.wait_ge(top_found, 1)
            for t in range(TT):
                ins = nc.vector.max_index(idx8[:, t, :], top8[:, t, :], logits[:, t, :])
                if t == 0:
                    ins.then_inc(top_found, 1)
            link(ins)
            dve.wait_ge(top_found, 2)
            nc.vector.tensor_scalar(ntop[:, :], top8[:, :, 0], -1.0, None, ALU.mult).then_inc(router_max, 1)
            link(nc.vector.tensor_copy(idx8f[:, :, :], idx8[:, :, :]))
            link(nc.vector.tensor_tensor(hits,
                                         iota_s[:, 0:NE].unsqueeze(1).unsqueeze(3).to_broadcast([P, TT, NE, TOPK]),
                                         idx8f[:, :, 0:TOPK].unsqueeze(2).to_broadcast([P, TT, NE, TOPK]),
                                         ALU.is_equal))
            with nc.allow_low_precision("a sum of at most one 1"):
                nc.vector.tensor_reduce(sel[:, :, :], hits, axis=AX_X, op=ALU.add).then_inc(chosen, 1)
            dve.wait_ge(chosen, 1)
            dve.wait_ge(ranked, 1)
            link(nc.vector.scalar_tensor_tensor(out=posm[:, :, 0:NE],
                                                in0=ps[:, 7, P:P + TT * NE].rearrange("p (t e) -> p t e", t=TT),
                                                scalar=1.0, in1=sel[:, :, :], op0=ALU.add, op1=ALU.mult))
            link(nc.vector.tensor_scalar_add(posm[:, :, 0:NE], posm[:, :, 0:NE], -1.0))
            moe_gain = gains[:, 3, :].unsqueeze(2).to_broadcast([P, KC, SLOTS])

            def one_hot(e, slots, done):
                for t in range(TT):
                    last = nc.vector.tensor_scalar(pick[:, t, :], slots, posm[:, t, bass.ds(e, 1)], None,
                                                   ALU.is_equal)
                last.then_inc(done, 1)

            one_hot(0, iota_s[:, 0:SLOTS], pick_ready)
            cnt = tabf[0:1, 0, :]
            dve.wait_ge(pick_ready, 1)
            link(nc.vector.tensor_copy(cnt, ps[0:1, 7, P + 2 * NE:P + 3 * NE]))
            link(nc.vector.tensor_scalar(tabf[0:1, 1, :], cnt, float(SLOTS), None, ALU.is_gt))
            for q in range(2, MAXBLK):
                link(nc.vector.scalar_tensor_tensor(out=tabf[0:1, 1, :], in0=cnt, scalar=float(q * SLOTS),
                                                    in1=tabf[0:1, 1, :], op0=ALU.is_gt, op1=ALU.add))
            link(nc.vector.memset(tabf[0:1, 2, :], 1.0))
            link(nc.vector.tensor_tensor_scan(tabf[0:1, 3, :], tabf[0:1, 2, :], tabf[0:1, 1, :], 0.0,
                                              ALU.mult, ALU.add))
            link(nc.vector.tensor_tensor(tabf[0:1, 4, :], tabf[0:1, 3, :], tabf[0:1, 1, :], ALU.subtract))
            link(nc.vector.tensor_copy(tab[0:1, 0, :], cnt))
            nc.vector.tensor_copy(tab[0:1, 1, :], tabf[0:1, 4, :]).then_inc(table_ready, 1)
            dve.wait_ge(router_exp, 2)
            for t in range(TT):
                link(nc.vector.tensor_tensor_reduce(out=elog[:, t, :], in0=elog[:, t, :], in1=sel[:, t, :],
                                                    scale=1.0, scalar=0.0, op0=ALU.mult, op1=ALU.add,
                                                    accum_out=gate_sum[:, t:t + 1]))
            link(nc.vector.reciprocal(gate_sum[:, :], gate_sum[:, :]))
            link(nc.vector.tensor_tensor(gates, elog[:, :, :], gate_sum[:, :].unsqueeze(2).to_broadcast([P, TT, NE]),
                                         ALU.mult))

            def one_hot_gated(e, slots, done):
                for t in range(TT):
                    for n in range(2):
                        last = nc.vector.tensor_scalar(pick_gated[:, t, n, :], slots, posm[:, t, bass.ds(e, 1)],
                                                       gates[:, t, bass.ds(e, 1)], ALU.is_equal, ALU.mult)
                last.then_inc(done, 1)

            def keep_gathered(dst, done):
                nc.vector.tensor_tensor(dst, ps[:, 6, :].rearrange("p (c s) -> p c s", c=KC), moe_gain,
                                        ALU.mult).then_inc(done, 1)

            h_pair = banks(4, 6).rearrange("p b (n two) -> p b n two", two=2)

            def as_banks(ap):
                return ap.rearrange("p (b n) -> p b n", b=2)

            nc.vector.tensor_copy(b1_pick, ident[:, 0:1].to_broadcast([P, SLOTS])).then_inc(b1_pick_ready, 1)
            dve.wait_ge(gathered, 1)
            keep_gathered(xgT, xgT_ready)

            dve.wait_ge(table_ready, 1)
            for free in (act_ready, y_ready):
                dve.sem_inc(free, 1)
            with dve.Fori(0, NE) as e:
                nc.vector.tensor_copy(b2_pick, ident[:, bass.ds(e, 1)].to_broadcast([P, SLOTS])).then_inc(
                    b2_pick_ready, 1)
                count = dve.value_load(tab[0:1, 0, bass.ds(e, 1)], min_val=0, max_val=T)
                with dve.If(count > SLOTS):
                    first = dve.value_load(tab[0:1, 1, bass.ds(e, 1)], min_val=0, max_val=NE)
                    with dve.Fori(1, MAXBLK) as q:
                        with dve.If(count > q * SLOTS):
                            n = first + q
                            slots = iota_s[:, bass.ds(q * SLOTS, SLOTS)]
                            dve.wait_ge(gathered, e + 1)
                            one_hot(e, slots, m_pick)
                            dve.wait_ge(pickg_turned, e + 1)
                            one_hot_gated(e, slots, m_pick)
                            dve.wait_ge(m_gathered, n)
                            keep_gathered(xgT_more, m_xgT)
                            dve.wait_ge(m_up, n)
                            nc.vector.tensor_scalar_min(as_banks(glu), h_pair[:, :, :, 0], LIMIT).then_inc(m_glu, 1)
                            nc.vector.tensor_scalar(as_banks(lin), h_pair[:, :, :, 1], LIMIT, -LIMIT, ALU.min,
                                                    ALU.max).then_inc(m_lin, 1)
                            dve.wait_ge(m_sig, n)
                            dve.wait_ge(m_lin, n)
                            nc.vector.scalar_tensor_tensor(out=lin, in0=lin, scalar=1.0, in1=sig, op0=ALU.add,
                                                           op1=ALU.mult).then_inc(m_dve, 1)
                            dve.wait_ge(m_dve, n)
                            dve.wait_ge(m_glu, n)
                            dve.wait_ge(act_turned, e + 1)
                            nc.vector.tensor_tensor(actb, lin, glu, ALU.mult).then_inc(m_act, 1)
                            dve.wait_ge(m_down, n)
                            dve.wait_ge(scattered, e + 1)
                            nc.vector.tensor_copy(y_sb, ps[:, 6, :]).then_inc(m_y, 1)
                            dve.wait_ge(m_scattered, n)
                            dve.sem_inc(m_closed, 1)
                dve.wait_ge(pickg_turned, e + 1)
                one_hot_gated(e, iota_s[:, 0:SLOTS], pickg_ready)
                dve.wait_ge(gathered, e + 1)
                one_hot(e + 1, iota_s[:, 0:SLOTS], pick_ready)
                dve.wait_ge(bias_added, e + 1)
                nc.vector.tensor_copy(b1_pick, ident[:, bass.ds(e + 1, 1)].to_broadcast([P, SLOTS])).then_inc(
                    b1_pick_ready, 1)
                dve.wait_ge(up_used, e * 8 + 8)
                nc.vector.tensor_scalar_min(as_banks(glu), h_pair[:, :, :, 0], LIMIT).then_inc(glu_ready, 1)
                nc.vector.tensor_scalar(as_banks(lin), h_pair[:, :, :, 1], LIMIT, -LIMIT, ALU.min,
                                        ALU.max).then_inc(dve_loop, 1)
                dve.wait_ge(sig_ready, e + 1)
                dve.wait_ge(dve_loop, e * 2 + 1)
                nc.vector.scalar_tensor_tensor(out=lin, in0=lin, scalar=1.0, in1=sig, op0=ALU.add,
                                               op1=ALU.mult).then_inc(dve_loop, 1)
                dve.wait_ge(dve_loop, e * 2 + 2)
                dve.wait_ge(glu_ready, e + 1)
                dve.wait_ge(act_turned, e + 1)
                nc.vector.tensor_tensor(actb, lin, glu, ALU.mult).then_inc(act_ready, 1)
                dve.wait_ge(gathered, e + 2)
                keep_gathered(xgT, xgT_ready)
                dve.wait_ge(down_used, e * 4 + 4)
                dve.wait_ge(scattered, e + 1)
                nc.vector.tensor_copy(y_sb, ps[:, 6, :]).then_inc(y_ready, 1)

            for t in range(TT):
                if t == 0:
                    dve.wait_ge(tile0_scattered, NE)
                else:
                    dve.wait_ge(scattered, NE + 1)
                for n in range(2):
                    cols = slice(n * GW, (n + 1) * GW)
                    nc.vector.tensor_tensor(h[:, t, cols], ps[:, 2 * t + n, :], h[:, t, cols],
                                            ALU.add).then_inc(residual_ready, 1)
            dve.wait_ge(residual_ready, 12)
            dve.wait_ge(lnf_loaded, 16)
            for t in range(TT):
                dve.wait_ge(std_ready, 8 + t + 1)
                link(nc.vector.reciprocal(rstd[:, t:t + 1], std[:, t:t + 1]))
                nc.vector.scalar_tensor_tensor(out=hn[:, t, :], in0=h[:, t, :], scalar=rstd[:, t:t + 1], in1=lnf,
                                               op0=ALU.mult, op1=ALU.mult).then_inc(rows_final, 1)

        @block.tensor
        def _(pe):
            def turn_rows(n, t, src):
                pe.wait_ge(hn_ready, 2 * n + t + 1)
                for half in range(2):
                    for c in range(4):
                        last = nc.tensor.transpose(ps[:, TURN_BANKS[n][t] + half, c * P:(c + 1) * P],
                                                   src[:, t, (4 * half + c) * P:(4 * half + c + 1) * P], ident[:, :])
                    last.then_inc(hn_turned, 1)

            def feature_quarter(g, m, bank, srcT):
                for k in range(KC):
                    last = nc.tensor.matmul(ps[:, bank + m // 2, (m % 2) * T:(m % 2 + 1) * T],
                                            group_unit(g, k)[:, m * P:(m + 1) * P], srcT[:, k, :],
                                            start=(k == 0), stop=(k == KC - 1))
                return last

            def token_quarter(g, j, bank, srcT, bank_step=1):
                t = j // 2
                for k in range(4 * (j % 2), 4 * (j % 2) + 4):
                    last = nc.tensor.matmul(ps[:, bank + t * bank_step, :], srcT[:, k, t * P:(t + 1) * P],
                                            group_unit(g, k), start=(k == 0), stop=(k == KC - 1))
                return last

            def group_start(g):
                group_arrived(pe, g, 0)
                group_arrived(pe, g, 1)

            def whole_group(g, bank, srcT):
                group_start(g)
                for m in range(4):
                    last = feature_quarter(g, m, bank, srcT)
                last.then_inc(group_done, 1)

            pe.wait_ge(consts_ready, 2)
            pe.wait_ge(small_loaded, 16 * 6)
            nc.tensor.transpose(ps[:, 0, 0:GAIN_ROWS], gain_rows, ident[0:GAIN_ROWS, 0:GAIN_ROWS]).then_inc(gains_turned, 1)
            for t in range(TT):
                turn_rows(0, t, hn)
            pe.wait_ge(gains_turned, 2)
            pe.wait_ge(hnT_ready, 4)
            whole_group(G_F, 0, hnT)
            whole_group(G_Q, 2, hnT)
            for t in range(TT):
                turn_rows(1, t, mem_n)
            pe.wait_ge(group_kept, G_F + 1)
            whole_group(M_Q, 0, hnT)
            pe.wait_ge(group_kept, G_Q + 1)
            whole_group(M_K, 2, hnT)
            pe.wait_ge(hnT_ready, 8)

            for item in order:
                kind, i = item[0], item[1]
                if kind == "proj":
                    j = item[2]
                    if j == 0:
                        pe.wait_ge(group_kept, M_Q + 1 if i == M_V else i)
                        group_start(i)
                    if i in FEATURE_GROUPS:
                        last = feature_quarter(i, j, 0, memT)
                    else:
                        last = token_quarter(i, j, 0, hnT if i <= G_G else memT)
                    if j == 3:
                        last.then_inc(group_done, 1)
                elif kind == "level":
                    pe.wait_ge(pad_ready, 2 * i + 2)
                    if i == 0:
                        pe.wait_ge(group_kept, M_K + 1)
                    else:
                        pe.wait_ge(level_kept, 2 * i)
                    stationary = (kgate if i == DIAG else factor[i % 2]).rearrange("p (c t) -> p c t", c=NPAIR)
                    for half in range(1 if i == OFF else 2):
                        for c in range(NPAIR):
                            s0 = half * P
                            t0 = P if i == OFF else s0
                            last = nc.tensor.matmul(
                                ps[:, 2 + 2 * half + c // 2, (c % 2) * T:(c % 2 + 1) * T],
                                stationary[:, c, s0:s0 + P], factor_pad[:, c, :, t0:t0 + P],
                                start=True, stop=True)
                        last.then_inc(level_done, 2 if i == OFF else 1)
                elif kind == "score":
                    if i == 0:
                        pe.wait_ge(group_kept, M_K + 1)
                    else:
                        pe.wait_ge(score_kept, i)
                    rows = slice(64 * (i % 2), 64 * (i % 2) + 64)
                    nc.tensor.matmul(ps[:, 6, 0:128], mqT[rows, i // 2, 0:P], mkT[rows, i // 2, 0:P],
                                     start=True, stop=True)
                    nc.tensor.matmul(ps[:, 6, 128:384], mqT[rows, i // 2, P:T], mkT[rows, i // 2, :],
                                     start=True, stop=True).then_inc(score_done, 1)
                elif kind == "turn":
                    pe.wait_ge(prob_ready, 2 * i + 2)
                    if i >= 1:
                        pe.wait_ge(head_kept, i)
                    for c in range(3):
                        last = nc.tensor.transpose(ps[:, 7, c * P:(c + 1) * P], mp(i)[:, c * P:(c + 1) * P], ident[:, :])
                    last.then_inc(prob_turned, 1)
                elif kind == "out":
                    pe.wait_ge(group_kept, M_V + 1)
                    pe.wait_ge(probT_ready, i + 1)
                    cols = slice(i * HD, (i + 1) * HD)
                    nc.tensor.matmul(ps[:, 7, 384:448], mpT(i)[:, 0:P], mv[:, 0, cols], start=True, stop=True)
                    nc.tensor.matmul(ps[:, 7, 448:512], mpT(i)[:, P:2 * P], mv[:, 0, cols], start=True, stop=False)
                    nc.tensor.matmul(ps[:, 7, 448:512], mpT(i)[:, 2 * P:3 * P], mv[:, 1, cols], start=False,
                                     stop=True).then_inc(head_done, 1)

            def turn_mix(half):
                for c in range(4 * half, 4 * half + 4):
                    for t in range(TT):
                        col = (c % 2) * T + t * P
                        last = nc.tensor.transpose(ps[:, 6 + c // 2 - 2 * half, col:col + P],
                                                   mix[:, t, c * P:(c + 1) * P], ident[:, :])
                last.then_inc(mix_turned, 1)

            pe.wait_ge(head_kept, NH)
            turn_mix(0)
            pe.wait_ge(level_kept, 2 * NLEV)
            a5 = a_in.rearrange("p (c n j t) -> p c n j t", c=NPAIR, n=2, j=2)
            o4 = a_off.rearrange("p (c j t) -> p c j t", c=NPAIR, j=2)
            for i in range(NH):
                c, j, cols = i // 2, i % 2, slice(i * HD, (i + 1) * HD)
                nc.tensor.matmul(ps[:, 4, cols], a5[:, c, 0, j, :], gi[:, 0, cols], start=True, stop=True)
                nc.tensor.matmul(ps[:, 5, cols], a5[:, c, 1, j, :], gi[:, 1, cols], start=True, stop=False)
                last = nc.tensor.matmul(ps[:, 5, cols], o4[:, c, j, :], gi[:, 0, cols], start=False, stop=True)
            last.then_inc(hg_done, 1)

            pe.wait_ge(group_kept, X_V0 + 1)
            pe.wait_ge(mixT_ready, 1)
            group_start(W_O0)
            group_start(W_O1)
            for n, g in enumerate((W_O0, W_O1)):
                for t in range(TT):
                    token_quarter(g, 2 * t, 2 * n, mixT)
            pe.wait_ge(hg_mix_ready, 1)
            turn_mix(1)
            group_start(X_V1)
            token_quarter(X_V1, 0, 4, memT)
            pe.wait_ge(mixT_ready, 2)
            for t in range(TT):
                for n, g in enumerate((W_O0, W_O1)):
                    last = token_quarter(g, 2 * t + 1, 2 * n, mixT)
                    last.then_inc(rows_done if t == 0 else group_done, 1)
            token_quarter(X_V1, 1, 4, memT)
            turn_rows(2, 0, hn)
            token_quarter(X_V1, 2, 4, memT)
            token_quarter(X_V1, 3, 4, memT).then_inc(group_done, 1)
            pe.wait_ge(residual_ready, 4)
            turn_rows(2, 1, hn)

            pe.wait_ge(hnT_ready, 12)
            whole_group(X_Q0, 2, hnT)
            group_start(X_Q1)
            group_start(C_O0)

            def more_queries(m):
                last = feature_quarter(X_Q1, m, 6, hnT)
                if m == 3:
                    last.then_inc(group_done, 1)

            def head_scores(i):
                pe.wait_ge(group_kept, kept_count(X_Q0 if i < 2 else X_Q1))
                if i >= 2:
                    pe.wait_ge(xs_prob, 2 * (i - 1))
                for t in range(TT):
                    for c in range(2):
                        last = nc.tensor.matmul(ps[:, i % 2, t * T:(t + 1) * T],
                                                qxT[:, 2 * i + c, t * P:(t + 1) * P], KxT[:, 2 * i + c, :],
                                                start=(c == 0), stop=(c == 1))
                last.then_inc(xs_done, 1)

            def turn_probs(n):
                pe.wait_ge(xs_scaled, 2 * n + 2)
                if n == 0:
                    pe.wait_ge(group_kept, kept_count(X_V1))
                else:
                    pe.wait_ge(xpT_ready, n)
                for t in range(TT):
                    for k in range(TT):
                        last = nc.tensor.transpose(ps[:, 4, k * T + t * P:k * T + (t + 1) * P],
                                                   xp(n)[:, t, k * P:(k + 1) * P], ident[:, :])
                last.then_inc(xp_turned, 1)

            def head_output(n):
                pe.wait_ge(xpT_ready, n + 1)
                if n >= 1:
                    pe.wait_ge(xo_kept, n)
                for c in range(2):
                    for k in range(TT):
                        last = nc.tensor.matmul(ps[:, 5, c * T:(c + 1) * T],
                                                Vx[:, k, (2 * n + c) * P:(2 * n + c + 1) * P], xpT[:, k, :],
                                                start=(k == 0), stop=(k == 1))
                last.then_inc(xo_done, 1)

            def project(n, q, t):
                for k in (2 * n, 2 * n + 1):
                    last = nc.tensor.matmul(ps[:, (6, 2)[q] + t, :], qxT[:, k, t * P:(t + 1) * P],
                                            group_unit(C_O0 + q, k), start=(k == 0), stop=(k == KC - 1))
                return last

            def project_tiles(n, q):
                for t in range(TT):
                    project(n, q, t)

            head_scores(0)
            more_queries(0)
            head_scores(1)
            more_queries(1)
            turn_probs(0)
            more_queries(2)
            head_output(0)
            more_queries(3)
            turn_probs(1)
            pe.wait_ge(xo_kept, 1)
            group_start(C_O1)
            project_tiles(0, 1)
            head_output(1)
            head_scores(2)
            project_tiles(0, 0)
            head_scores(3)
            turn_probs(2)
            pe.wait_ge(xo_kept, 2)
            project_tiles(1, 0)
            head_output(2)
            project_tiles(1, 1)
            turn_probs(3)
            pe.wait_ge(xo_kept, 3)
            project_tiles(2, 0)
            head_output(3)
            project_tiles(2, 1)
            pe.wait_ge(xo_kept, 4)
            for t in range(TT):
                for q in range(2):
                    project(3, q, t).then_inc(rows_done if t == 0 else group_done, 1)

            for t in range(TT):
                turn_rows(3, t, hn)
            pe.wait_ge(hnT_ready, 16)
            pe.wait_ge(router_loaded, 32)
            pe.wait_ge(masks_ready, 9)
            for k in range(KC):
                j = k % 2
                last = nc.tensor.matmul(ps[64 * j:64 * j + 64, 6, 0:T], wr[:, k, :], hnT[:, k, :],
                                        start=(k < 2), stop=(k >= KC - 2))
            last.then_inc(router_done, 1)
            pe.wait_ge(logitsT_ready, 1)
            for t in range(TT):
                last = nc.tensor.matmul(ps[:, 7, t * NE:(t + 1) * NE], logitsT[:, t * P:(t + 1) * P], fold[:, :],
                                        start=True, stop=True)
            last.then_inc(logits_done, 1)
            pe.wait_ge(loop_zeroed, 7)
            for bank in range(4):
                nc.tensor.matmul(ps[:, bank, :], zeros_b[:, 0:P], zeros_b,
                                 start=True, stop=False, skip_group_check=True)
            pe.wait_ge(chosen, 1)
            nc.tensor.matmul(ps[:, 7, P:P + NE], before_b[:, :], sel[:, 0, :], start=True, stop=True)
            nc.tensor.matmul(ps[:, 7, P + NE:P + 2 * NE], ones_b[:, :], sel[:, 0, :], start=True, stop=False)
            nc.tensor.matmul(ps[:, 7, P + NE:P + 2 * NE], before_b[:, :], sel[:, 1, :], start=False, stop=True)
            nc.tensor.matmul(ps[:, 7, P + 2 * NE:P + 3 * NE], ones_b[:, :], sel[:, 0, :], start=True, stop=False)
            nc.tensor.matmul(ps[:, 7, P + 2 * NE:P + 3 * NE], ones_b[:, :], sel[:, 1, :], start=False,
                             stop=True).then_inc(ranked, 1)

            def gather(done):
                for c in range(KC):
                    n = 0
                    for part in xn_part:
                        for t in range(TT):
                            last = nc.tensor.matmul(ps[:, 6, c * SLOTS:(c + 1) * SLOTS],
                                                    part[:, t, c * P:(c + 1) * P], pick[:, t, :],
                                                    start=(n == 0), stop=(n == 5))
                            n += 1
                last.then_inc(done, 1)

            def turn_gated(done):
                for t in range(TT):
                    last = nc.tensor.transpose(ps[:, 7, t * P:(t + 1) * P],
                                               pick_gated[:, t, :, :].rearrange("p n s -> p (n s)"), ident[:, :])
                last.then_inc(done, 1)

            def bias_up():
                for c in range(2):
                    for j in range(2):
                        last = nc.tensor.matmul(ps[64 * j:64 * j + 64, 4 + c, :], b1_pick,
                                                b1_sb[:, j * 1024 + c * GW:j * 1024 + (c + 1) * GW],
                                                start=True, stop=False)
                return last

            def up_unit(src, k):
                for c in range(2):
                    for j in range(2):
                        last = nc.tensor.matmul(ps[64 * j:64 * j + 64, 4 + c, :], src[:, k, :],
                                                expert_ring[:, k, j * 1024 + c * GW:j * 1024 + (c + 1) * GW],
                                                start=False, stop=(k == KC - 1))
                return last

            def turn_act(done):
                for q in range(4):
                    last = nc.tensor.transpose(ps[:, 7, q * P:(q + 1) * P], actb[:, q * P:(q + 1) * P], ident[:, :])
                last.then_inc(done, 1)

            def bias_down():
                for n in range(2):
                    nc.tensor.matmul(ps[64 * n:64 * n + 64, 6, :], b2_pick, b2_sb[:, n * GW:(n + 1) * GW],
                                     start=True, stop=False)

            def down_unit(odd, v):
                slot = odd_slot[v] if odd else expert_ring[:, 8 + v, :]
                for a in range(2):
                    kk = 2 * v + a
                    for n in range(2):
                        last = nc.tensor.matmul(ps[64 * n:64 * n + 64, 6, :], actT[:, kk % 4, kk // 4, :],
                                                slot[:, a * D + n * GW:a * D + (n + 1) * GW],
                                                start=False, stop=(kk == 7))
                return last

            def scatter(done, tile0_done=None):
                for t in range(TT):
                    for n in range(2):
                        last = nc.tensor.matmul(ps[:, 2 * t + n, :], sgT[:, n, t * P:(t + 1) * P], y_sb,
                                                start=False, stop=False, skip_group_check=True)
                    if t == 0 and tile0_done is not None:
                        last.then_inc(tile0_done, 1)
                last.then_inc(done, 1)

            def wait_up_unit(e, k):
                pe.wait_ge(expert_loaded[k], e * 16 + 16)

            def wait_down_unit(pair, odd, v):
                pe.wait_ge(odd_loaded[v] if odd else expert_loaded[8 + v], pair * 16 + 16)

            def further_blocks(pair, odd, e, count):
                with pe.If(count > SLOTS):
                    first = pe.value_load(tab[0:1, 1, bass.ds(e, 1)], min_val=0, max_val=NE)
                    with pe.Fori(1, MAXBLK) as q:
                        with pe.If(count > q * SLOTS):
                            n = first + q
                            pe.wait_ge(m_pick, n * 2)
                            pe.wait_ge(xgT_ready, e + 1)
                            pe.wait_ge(y_ready, e + 1)
                            gather(m_gathered)
                            pe.wait_ge(actT_ready, e + 1)
                            turn_gated(m_turned)
                            pe.wait_ge(b1_pick_ready, e + 1)
                            pe.wait_ge(act_ready, e + 1)
                            bias_up()
                            pe.wait_ge(m_xgT, n)
                            for k in range(KC):
                                wait_up_unit(e, k)
                                last = up_unit(xgT_more, k)
                            last.then_inc(m_up, 1)
                            pe.wait_ge(m_act, n)
                            pe.wait_ge(m_sgT, n)
                            turn_act(m_actturn)
                            pe.wait_ge(m_actT, n)
                            pe.wait_ge(b2_pick_ready, e + 1)
                            bias_down()
                            for v in range(4):
                                wait_down_unit(pair, odd, v)
                                last = down_unit(odd, v)
                            last.then_inc(m_down, 1)
                            pe.wait_ge(m_y, n)
                            scatter(m_scattered)

            for t in range(TT):
                pe.wait_ge(rest_ready[t], 2)
                pe.wait_ge(part_ready[t], 2)
            pe.wait_ge(pick_ready, 1)
            pe.wait_ge(loop_zeroed, 7)
            pe.wait_ge(bias_loaded, 32)
            gather(gathered)
            pe.wait_ge(table_ready, 1)
            for free in (pickg_turned, act_turned, scattered):
                pe.sem_inc(free, 1)
            with pe.Fori(0, NE // 2) as pair:
                for odd in range(2):
                    e = pair * 2 + odd
                    count = pe.value_load(tab[0:1, 0, bass.ds(e, 1)], min_val=0, max_val=T)
                    further_blocks(pair, odd, e, count)
                    pe.wait_ge(b1_pick_ready, e + 1)
                    pe.wait_ge(act_ready, e + 1)
                    bias_up().then_inc(bias_added, 1)
                    pe.wait_ge(xgT_ready, e + 1)
                    for k in range(KC):
                        wait_up_unit(e, k)
                        up_unit(xgT, k).then_inc(up_used, 1)
                    pe.wait_ge(pick_ready, e + 2)
                    pe.wait_ge(y_ready, e + 1)
                    gather(gathered)
                    pe.wait_ge(pickg_ready, e + 1)
                    pe.wait_ge(actT_ready, e + 1)
                    turn_gated(pickg_turned)
                    pe.wait_ge(act_ready, e + 2)
                    pe.wait_ge(sgT_ready, e + 1)
                    turn_act(act_turned)
                    pe.wait_ge(xgT_ready, e + 2)
                    pe.wait_ge(b2_pick_ready, e + 1)
                    bias_down()
                    pe.wait_ge(actT_ready, e + 2)
                    for v in range(4):
                        wait_down_unit(pair, odd, v)
                        down_unit(odd, v).then_inc(down_used, 1)
                    pe.wait_ge(y_ready, e + 2)
                    scatter(scattered, tile0_scattered)


_INS = ['x', 'mem', 'ln_mix_g', 'w_in', 'hgrn_lb_logits', 'hgrn_norm_g', 'w_out', 'ln_x_g', 'ln_mem_g', 'wq_x',
        'wkv_x', 'wo_x', 'ln_moe_g', 'w_router', 'b_router', 'w1', 'b1', 'w2', 'b2', 'ln_f_g']


def kernel(**inputs):
    import concourse.bacc as _bacc
    from concourse.bass_utils import run_bass_kernel_spmd as _run

    nc = _bacc.Bacc("TRN2", target_bir_lowering=False, num_devices=1)
    arrays, args = {}, []
    for name in _INS:
        a = np.ascontiguousarray(inputs[name])
        arrays[f"in_{name}_dram"] = a
        args.append(nc.dram_tensor(f"in_{name}_dram", a.shape, mybir.dt.from_np(a.dtype), kind="ExternalInput").ap())
    args.append(nc.dram_tensor("out_0_dram", (1, T, D), F32, kind="ExternalOutput").ap())
    build(nc, *args)
    r = _run(nc, [arrays], core_ids=[0])
    return r.results[0]["out_0_dram"]
```
